# Optimizing a Trainium2 kernel written in Bass

```python
import math
import jax, jax.numpy as jnp
from jax import lax
import numpy as np
import jax
import jax.numpy as jnp

D_MODEL = 1024
BATCH = 1
SEQ = 512
DEPTH = 1

D_MIX = D_MODEL
CONV_WIDTH = D_MIX // 2
CONV_GROUPS = 8
CONV_K = 3
DN_WIDTH = D_MIX - CONV_WIDTH
DN_HEADS = 4
DN_HEAD_DIM = DN_WIDTH // DN_HEADS
DN_CONV_K = 4
DN_CHUNK = 64
IN_COLS = 3 * CONV_WIDTH + 4 * DN_WIDTH + 2 * DN_HEADS
MEM_LEN = 256
X_HEADS = 4
X_HEAD_DIM = D_MODEL // X_HEADS
PEER_HEADS = 8
PEER_KEYS = 128
PEER_EXPERTS = PEER_KEYS * PEER_KEYS
PEER_TOPK = 16
PEER_QDIM = 128
PEER_HALF = PEER_QDIM // 2
PEER_BLOCK = 128
EPS = 1e-6


def rms_norm(x, gain, eps=EPS):
    xf = x.astype(jnp.float32)
    y = xf * lax.rsqrt(jnp.mean(xf * xf, axis=-1, keepdims=True) + eps)
    return (y * gain.astype(jnp.float32)).astype(x.dtype)

def l2_normalize(t, eps=EPS):
    tf = t.astype(jnp.float32)
    return tf * lax.rsqrt(jnp.sum(tf * tf, axis=-1, keepdims=True) + eps)

def causal_depthwise_conv(x, w):
    k = w.shape[0]
    return lax.conv_general_dilated(
        x, w[:, None, :].astype(x.dtype), window_strides=(1,), padding=[(k - 1, 0)],
        dimension_numbers=("NWC", "WIO", "NWC"), feature_group_count=x.shape[-1])

def chunk_gated_delta_rule(q, k, v, g, beta):
    f32 = jnp.float32
    bsz, seq, nh, dk = q.shape
    dv = v.shape[-1]
    nc = seq // DN_CHUNK

    def to_chunks(t):
        t = t.astype(f32).reshape(bsz, nc, DN_CHUNK, nh, *t.shape[3:])
        return jnp.moveaxis(t, 3, 1)

    q = to_chunks(q) * (dk ** -0.5)
    k = to_chunks(k)
    v = to_chunks(v)
    beta = to_chunks(beta)
    g = jnp.cumsum(to_chunks(g), axis=-1)

    causal = jnp.tril(jnp.ones((DN_CHUNK, DN_CHUNK), dtype=bool))
    strict = jnp.tril(jnp.ones((DN_CHUNK, DN_CHUNK), dtype=bool), -1)
    diff = g[..., :, None] - g[..., None, :]
    decay = jnp.where(causal, jnp.exp(jnp.where(causal, diff, 0.0)), 0.0)

    k_beta = k * beta[..., None]
    v_beta = v * beta[..., None]
    a = jnp.where(strict, jnp.einsum("bhnid,bhnjd->bhnij", k_beta, k) * decay, 0.0)
    eye = jnp.eye(DN_CHUNK, dtype=f32)
    t_mat = lax.linalg.triangular_solve(a + eye, jnp.broadcast_to(eye, a.shape),
                                        left_side=True, lower=True, unit_diagonal=True)
    u = jnp.einsum("bhnij,bhnjd->bhnid", t_mat, v_beta)
    w = jnp.einsum("bhnij,bhnjd->bhnid", t_mat, k_beta * jnp.exp(g)[..., None])
    intra = jnp.einsum("bhnid,bhnjd->bhnij", q, k) * decay
    q_dec = q * jnp.exp(g)[..., None]
    k_dec = k * jnp.exp(g[..., -1:] - g)[..., None]
    g_last = jnp.exp(g[..., -1])

    xs = tuple(jnp.moveaxis(t, 2, 0) for t in (q_dec, k_dec, u, w, intra, g_last))

    def step(state, inp):
        q_c, k_c, u_c, w_c, a_c, gl = inp
        v_new = u_c - jnp.einsum("bhcd,bhde->bhce", w_c, state)
        o = jnp.einsum("bhcd,bhde->bhce", q_c, state) + jnp.einsum("bhij,bhje->bhie", a_c, v_new)
        state = state * gl[..., None, None] + jnp.einsum("bhcd,bhce->bhde", k_c, v_new)
        return state, o

    s0 = jnp.zeros((bsz, nh, dk, dv), f32)
    _, o = lax.scan(step, s0, xs)
    return o.transpose(1, 0, 3, 2, 4).reshape(bsz, seq, nh, dv)

def hybrid_mixer(xn, w_in, conv_w, dn_conv_w, dn_a_log, dn_dt_bias, dn_norm, w_out):
    bsz, seq, _ = xn.shape
    proj = xn @ w_in
    o1 = CONV_WIDTH
    o2 = 2 * CONV_WIDTH
    o3 = 3 * CONV_WIDTH
    o4 = o3 + 3 * DN_WIDTH
    o5 = o4 + DN_WIDTH
    o6 = o5 + DN_HEADS
    b_gate, c_gate, h_conv, qkv, z, beta_logit, a_logit = jnp.split(
        proj, [o1, o2, o3, o4, o5, o6], axis=-1)

    y_conv = b_gate * causal_depthwise_conv(c_gate * h_conv, conv_w)

    qkv = jax.nn.silu(causal_depthwise_conv(qkv, dn_conv_w))
    q, k, v = jnp.split(qkv, 3, axis=-1)
    hs = (bsz, seq, DN_HEADS, DN_HEAD_DIM)
    q = l2_normalize(q.reshape(hs))
    k = l2_normalize(k.reshape(hs))
    v = v.reshape(hs)
    beta = jax.nn.sigmoid(beta_logit.astype(jnp.float32))
    g = -jnp.exp(dn_a_log.astype(jnp.float32)) * jax.nn.softplus(
        a_logit.astype(jnp.float32) + dn_dt_bias.astype(jnp.float32))
    o = chunk_gated_delta_rule(q, k, v, g, beta)
    o = rms_norm(o, dn_norm) * jax.nn.silu(z.reshape(hs).astype(jnp.float32))
    y_dn = o.reshape(bsz, seq, DN_WIDTH).astype(xn.dtype)

    return jnp.concatenate([y_conv, y_dn], axis=-1) @ w_out

def memory_cross_attention(xn, mem_n, w_q, w_kv, w_o):
    bsz, seq, _ = xn.shape
    q = (xn @ w_q).reshape(bsz, seq, X_HEADS, X_HEAD_DIM)
    kv = (mem_n @ w_kv).reshape(bsz, mem_n.shape[1], 2, X_HEADS, X_HEAD_DIM)
    k, v = kv[:, :, 0], kv[:, :, 1]
    s = jnp.einsum("bshd,bmhd->bhsm", q, k).astype(jnp.float32) * (X_HEAD_DIM ** -0.5)
    p = jax.nn.softmax(s, axis=-1).astype(xn.dtype)
    o = jnp.einsum("bhsm,bmhd->bshd", p, v).reshape(bsz, seq, D_MODEL)
    return o @ w_o

def peer_ffn(xn, w_query, sub_keys, expert_u, expert_v):
    bsz, seq, d = xn.shape
    q = (xn @ w_query).reshape(bsz, seq, PEER_HEADS, 2, PEER_HALF)
    scores = jnp.einsum("bshpd,hpnd->bshpn", q, sub_keys).astype(jnp.float32)
    s_top, i_top = lax.top_k(scores, PEER_TOPK)
    cand = (s_top[..., 0, :, None] + s_top[..., 1, None, :]).reshape(
        bsz, seq, PEER_HEADS, PEER_TOPK * PEER_TOPK)
    cand_idx = (i_top[..., 0, :, None] * PEER_KEYS + i_top[..., 1, None, :]).reshape(
        bsz, seq, PEER_HEADS, PEER_TOPK * PEER_TOPK)
    best, pos = lax.top_k(cand, PEER_TOPK)
    idx = jnp.take_along_axis(cand_idx, pos, axis=-1)
    gates = jax.nn.softmax(best, axis=-1).astype(xn.dtype)

    n_blk = (bsz * seq) // PEER_BLOCK
    sel = PEER_HEADS * PEER_TOPK
    xb = xn.reshape(n_blk, PEER_BLOCK, d)
    ib = idx.reshape(n_blk, PEER_BLOCK, sel)
    gb = gates.reshape(n_blk, PEER_BLOCK, sel)

    def block(args):
        xt, it, gt = args
        u = expert_u[it]
        v = expert_v[it]
        act = jax.nn.gelu(jnp.einsum("td,ted->te", xt, u), approximate=False)
        return jnp.einsum("te,ted->td", gt * act, v)

    y = lax.map(block, (xb, ib, gb))
    return y.reshape(bsz, seq, d)

def first_inputs(seed: int = 0) -> dict:
    key = jax.random.key(seed)
    ks = iter(jax.random.split(key, 32))
    f32 = jnp.float32
    L = DEPTH

    def nrm(shape, scale):
        return jax.random.normal(next(ks), shape, f32) * scale

    def gain(shape):
        return 1.0 + 0.02 * jax.random.normal(next(ks), shape, f32)

    x = nrm((BATCH, SEQ, D_MODEL), 1.0)
    mem = nrm((BATCH, MEM_LEN, D_MODEL), 1.0)
    norm_mix = gain((L, D_MODEL))
    w_in = nrm((L, D_MODEL, IN_COLS), D_MODEL ** -0.5)
    conv_w = nrm((L, CONV_K, CONV_WIDTH), CONV_K ** -0.5)
    dn_conv_w = nrm((L, DN_CONV_K, 3 * DN_WIDTH), DN_CONV_K ** -0.5)
    dn_a_log = jnp.log(jax.random.uniform(next(ks), (L, DN_HEADS), f32, 1.0, 16.0))
    dt = jnp.exp(jax.random.uniform(next(ks), (L, DN_HEADS), f32,
                                    math.log(1e-3), math.log(1e-1)))
    dn_dt_bias = dt + jnp.log(-jnp.expm1(-dt))
    dn_norm = gain((L, DN_HEAD_DIM))
    w_out = nrm((L, D_MIX, D_MODEL), D_MIX ** -0.5)
    norm_x = gain((L, D_MODEL))
    norm_mem = gain((L, D_MODEL))
    w_xq = nrm((L, D_MODEL, D_MODEL), D_MODEL ** -0.5)
    w_xkv = nrm((L, D_MODEL, 2 * D_MODEL), D_MODEL ** -0.5)
    w_xo = nrm((L, D_MODEL, D_MODEL), D_MODEL ** -0.5)
    norm_ffn = gain((L, D_MODEL))
    w_pq = nrm((L, D_MODEL, PEER_HEADS * PEER_QDIM), D_MODEL ** -0.5)
    peer_keys = nrm((L, PEER_HEADS, 2, PEER_KEYS, PEER_HALF), PEER_HALF ** -0.5)
    expert_u = nrm((L, PEER_EXPERTS, D_MODEL), D_MODEL ** -0.5)
    expert_v = nrm((L, PEER_EXPERTS, D_MODEL), PEER_TOPK ** -0.5)
    norm_final = gain((D_MODEL,))
    return {"x": x, "mem": mem, "norm_mix": norm_mix, "w_in": w_in, "conv_w": conv_w,
            "dn_conv_w": dn_conv_w, "dn_a_log": dn_a_log, "dn_dt_bias": dn_dt_bias,
            "dn_norm": dn_norm, "w_out": w_out, "norm_x": norm_x, "norm_mem": norm_mem,
            "w_xq": w_xq, "w_xkv": w_xkv, "w_xo": w_xo, "norm_ffn": norm_ffn,
            "w_pq": w_pq, "peer_keys": peer_keys, "expert_u": expert_u,
            "expert_v": expert_v, "norm_final": norm_final}

def first_block(x, mem, norm_mix, w_in, conv_w, dn_conv_w, dn_a_log, dn_dt_bias, dn_norm,
              w_out, norm_x, norm_mem, w_xq, w_xkv, w_xo, norm_ffn, w_pq, peer_keys,
              expert_u, expert_v, norm_final):
    h = x
    for layer in range(DEPTH):
        h = h + hybrid_mixer(rms_norm(h, norm_mix[layer]), w_in[layer], conv_w[layer],
                             dn_conv_w[layer], dn_a_log[layer], dn_dt_bias[layer],
                             dn_norm[layer], w_out[layer])
        h = h + memory_cross_attention(rms_norm(h, norm_x[layer]),
                                       rms_norm(mem, norm_mem[layer]),
                                       w_xq[layer], w_xkv[layer], w_xo[layer])
        h = h + peer_ffn(rms_norm(h, norm_ffn[layer]), w_pq[layer], peer_keys[layer],
                         expert_u[layer], expert_v[layer])
    return rms_norm(h, norm_final)


PLE_DIM = 256
NSA_HEADS = 8
NSA_KV_GROUPS = 2
NSA_REP = NSA_HEADS // NSA_KV_GROUPS
NSA_HEAD_DIM = 64
NSA_WIDTH = NSA_HEADS * NSA_HEAD_DIM
CMP_BLOCK = 32
CMP_STRIDE = 16
SEL_BLOCK = 64
N_SEL = 16
WINDOW = 512
SEL_Q_CHUNK = 16
MLA_HEADS = 8
Q_LORA = 256
KV_LORA = 128
QK_NOPE = 64
QK_ROPE = 32
V_DIM = 64
MLA_WIDTH = MLA_HEADS * V_DIM
ROPE_THETA = 10000.0
MAX_POS_OFFSET = 4096
D_FF = 2816
CONV_WIDTH_2 = 3
Q_BLOCK = 128
NEG = -1e30
BIG = 1e9
IN_SIZES = (NSA_WIDTH, 6 * NSA_KV_GROUPS * NSA_HEAD_DIM, 3 * NSA_HEADS, Q_LORA, KV_LORA, QK_ROPE, 2 * D_MODEL)
N_IN = NSA_WIDTH + 6 * NSA_KV_GROUPS * NSA_HEAD_DIM + 3 * NSA_HEADS + Q_LORA + KV_LORA + QK_ROPE + 2 * D_MODEL


def _rmsnorm(x, g):
    xf = x.astype(jnp.float32)
    y = xf * lax.rsqrt(jnp.mean(xf * xf, axis=-1, keepdims=True) + EPS)
    return (y * g.astype(jnp.float32)).astype(x.dtype)

def _masked_softmax(s, mask):
    p = jax.nn.softmax(jnp.where(mask, s, NEG), axis=-1)
    return p * mask.astype(p.dtype)

def _alibi_slopes(n):
    return jnp.asarray(np.array([2.0 ** (-8.0 * (i + 1) / n) for i in range(n)], dtype=np.float32))

def _rope(x, cos, sin):
    half = x.shape[-1] // 2
    x1, x2 = x[..., :half], x[..., half:]
    return jnp.concatenate([x1 * cos - x2 * sin, x2 * cos + x1 * sin], axis=-1)

def _causal_dwconv(u, w, b):
    c = u.shape[-1]
    y = lax.conv_general_dilated(u, w[:, None, :].astype(u.dtype), window_strides=(1,), padding=[(CONV_WIDTH_2 - 1, 0)], dimension_numbers=('NWC', 'WIO', 'NWC'), feature_group_count=c)
    return y + b

def _nsa_mixer(q, kc, vc, ks, vs, kw, vw, gates, pos_k, pos_v, ck_w1, ck_b1, ck_w2, cv_w1, cv_b1, cv_w2):
    B, T = q.shape[0], q.shape[1]
    G, R, dh = NSA_KV_GROUPS, NSA_REP, NSA_HEAD_DIM
    scale = dh ** -0.5
    slopes = _alibi_slopes(NSA_HEADS).reshape(G, R)
    t_idx = jnp.arange(T)

    n_cmp = (T - CMP_BLOCK) // CMP_STRIDE + 1
    blk = jnp.arange(n_cmp)[:, None] * CMP_STRIDE + jnp.arange(CMP_BLOCK)[None, :]

    def compress(k, pos, w1, b1, w2):
        kb = k[:, blk] + pos[None, None, :, None, :]
        kb = kb.transpose(0, 1, 3, 2, 4).reshape(B, n_cmp, G, CMP_BLOCK * dh)
        return jax.nn.gelu(kb @ w1 + b1) @ w2

    k_cmp = compress(kc, pos_k, ck_w1, ck_b1, ck_w2)
    v_cmp = compress(vc, pos_v, cv_w1, cv_b1, cv_w2)
    blk_end = jnp.arange(n_cmp) * CMP_STRIDE + CMP_BLOCK - 1
    dist_c = (t_idx[:, None] - blk_end[None, :]).astype(jnp.float32)
    s_c = jnp.einsum('btgrd,bjgd->bgrtj', q, k_cmp, preferred_element_type=jnp.float32) * scale
    s_c = s_c - slopes[:, :, None, None] * dist_c
    p_cmp = _masked_softmax(s_c, dist_c >= 0)
    o_cmp = jnp.einsum('bgrtj,bjgd->btgrd', p_cmp.astype(v_cmp.dtype), v_cmp)

    n_sb = T // SEL_BLOCK
    per = SEL_BLOCK // CMP_STRIDE
    imp = p_cmp.sum(axis=2)
    imp = jnp.pad(imp, ((0, 0), (0, 0), (0, 0), (0, n_sb * per - n_cmp)))
    imp = imp.reshape(B, G, T, n_sb, per).sum(axis=-1)
    cur = t_idx // SEL_BLOCK
    sb = jnp.arange(n_sb)
    forced = (sb[None, :] == 0) | (sb[None, :] == cur[:, None]) | (sb[None, :] == cur[:, None] - 1)
    future = sb[None, :] > cur[:, None]
    score = jnp.where(forced, BIG, jnp.where(future, -BIG, imp))
    k_sel = min(N_SEL, n_sb)
    _, sel_idx = lax.top_k(score, k_sel)

    ksb = ks.reshape(B, n_sb, SEL_BLOCK, G, dh).transpose(0, 3, 1, 2, 4)
    vsb = vs.reshape(B, n_sb, SEL_BLOCK, G, dh).transpose(0, 3, 1, 2, 4)
    C = SEL_Q_CHUNK
    n_ch = T // C
    q_ch = q.reshape(B, n_ch, C, G, R, dh).transpose(1, 0, 2, 3, 4, 5)
    idx_ch = sel_idx.reshape(B, G, n_ch, C, k_sel).transpose(2, 0, 1, 3, 4)
    t_ch = t_idx.reshape(n_ch, C)
    gather = jax.vmap(jax.vmap(lambda kb, ix: kb[ix]))

    def sel_step(args):
        qc, ic, tc = args
        kg = gather(ksb, ic)
        vg = gather(vsb, ic)
        s = jnp.einsum('bcgrd,bgckld->bgrckl', qc, kg, preferred_element_type=jnp.float32) * scale
        spos = ic[..., None] * SEL_BLOCK + jnp.arange(SEL_BLOCK)
        dist = (tc[None, None, :, None, None] - spos).astype(jnp.float32)
        s = s - slopes[None, :, :, None, None, None] * dist[:, :, None]
        s = s.reshape(B, G, R, C, k_sel * SEL_BLOCK)
        mask = (dist >= 0).reshape(B, G, 1, C, k_sel * SEL_BLOCK)
        pr = _masked_softmax(s, mask).reshape(B, G, R, C, k_sel, SEL_BLOCK)
        return jnp.einsum('bgrckl,bgckld->bcgrd', pr.astype(vg.dtype), vg)

    o_sel = lax.map(sel_step, (q_ch, idx_ch, t_ch))
    o_sel = o_sel.transpose(1, 0, 2, 3, 4, 5).reshape(B, T, G, R, dh)

    n_qb = T // Q_BLOCK
    span = WINDOW + Q_BLOCK
    kw_p = jnp.pad(kw, ((0, 0), (WINDOW, 0), (0, 0), (0, 0)))
    vw_p = jnp.pad(vw, ((0, 0), (WINDOW, 0), (0, 0), (0, 0)))
    q_blk = q.reshape(B, n_qb, Q_BLOCK, G, R, dh).transpose(1, 0, 2, 3, 4, 5)

    def win_step(args):
        qb, i = args
        start = i * Q_BLOCK
        kblk = lax.dynamic_slice_in_dim(kw_p, start, span, axis=1)
        vblk = lax.dynamic_slice_in_dim(vw_p, start, span, axis=1)
        tq = start + jnp.arange(Q_BLOCK)
        sk = start - WINDOW + jnp.arange(span)
        dist = (tq[:, None] - sk[None, :]).astype(jnp.float32)
        mask = (dist >= 0) & (dist < WINDOW) & (sk[None, :] >= 0)
        s = jnp.einsum('bqgrd,bsgd->bgrqs', qb, kblk, preferred_element_type=jnp.float32) * scale
        s = s - slopes[:, :, None, None] * dist
        pr = _masked_softmax(s, mask)
        return jnp.einsum('bgrqs,bsgd->bqgrd', pr.astype(vblk.dtype), vblk)

    o_win = lax.map(win_step, (q_blk, jnp.arange(n_qb, dtype=jnp.int32)))
    o_win = o_win.transpose(1, 0, 2, 3, 4, 5).reshape(B, T, G, R, dh)

    g = jax.nn.sigmoid(gates.astype(jnp.float32)).astype(q.dtype).reshape(B, T, 3, G, R, 1)
    o = g[:, :, 0] * o_cmp + g[:, :, 1] * o_sel + g[:, :, 2] * o_win
    return o.reshape(B, T, NSA_WIDTH)

def _mla_mixer(c_q, c_kv, k_rope, cos, sin, g_q, w_uq, g_kv, w_ukv):
    B, T = c_q.shape[0], c_q.shape[1]
    H = MLA_HEADS
    q = (_rmsnorm(c_q, g_q) @ w_uq).reshape(B, T, H, QK_NOPE + QK_ROPE)
    q_nope = q[..., :QK_NOPE]
    q_rope = _rope(q[..., QK_NOPE:], cos[:, :, None, :], sin[:, :, None, :])
    kv = (_rmsnorm(c_kv, g_kv) @ w_ukv).reshape(B, T, H, QK_NOPE + V_DIM)
    k_nope = kv[..., :QK_NOPE]
    v = kv[..., QK_NOPE:]
    k_r = _rope(k_rope, cos, sin)
    scale = (QK_NOPE + QK_ROPE) ** -0.5
    n_qb = T // Q_BLOCK
    qn_b = q_nope.reshape(B, n_qb, Q_BLOCK, H, QK_NOPE).transpose(1, 0, 2, 3, 4)
    qr_b = q_rope.reshape(B, n_qb, Q_BLOCK, H, QK_ROPE).transpose(1, 0, 2, 3, 4)
    s_idx = jnp.arange(T)

    def step(args):
        qn, qr, i = args
        s = (jnp.einsum('bqhd,bshd->bhqs', qn, k_nope, preferred_element_type=jnp.float32) + jnp.einsum('bqhd,bsd->bhqs', qr, k_r, preferred_element_type=jnp.float32)) * scale
        tq = i * Q_BLOCK + jnp.arange(Q_BLOCK)
        pr = _masked_softmax(s, s_idx[None, :] <= tq[:, None])
        return jnp.einsum('bhqs,bshd->bqhd', pr.astype(v.dtype), v)

    o = lax.map(step, (qn_b, qr_b, jnp.arange(n_qb, dtype=jnp.int32)))
    return o.transpose(1, 0, 2, 3, 4).reshape(B, T, MLA_WIDTH)

def second_inputs(seed: int = 0) -> dict:
    key = jax.random.key(seed)
    ks = jax.random.split(key, 40)
    f32 = jnp.float32

    def nrm(k, shape, fan_in):
        return jax.random.normal(k, shape, f32) * (fan_in ** -0.5)

    def gain(k, n):
        return 1.0 + 0.05 * jax.random.normal(k, (DEPTH, n), f32)

    def small(k, shape, s):
        return s * jax.random.normal(k, shape, f32)

    L = DEPTH
    dh = NSA_HEAD_DIM
    offs = jax.random.randint(ks[2], (BATCH, 1), 0, MAX_POS_OFFSET, dtype=jnp.int32)
    return {
        'x': jax.random.normal(ks[0], (BATCH, SEQ, D_MODEL), f32),
        'p': jax.random.normal(ks[1], (DEPTH, BATCH, SEQ, PLE_DIM), f32),
        'positions': offs + jnp.arange(SEQ, dtype=jnp.int32)[None, :],
        'g_pre_mix': gain(ks[3], D_MODEL),
        'w_in': nrm(ks[4], (L, D_MODEL, N_IN), D_MODEL),
        'nsa_pos_k': small(ks[5], (L, CMP_BLOCK, dh), 0.1),
        'nsa_pos_v': small(ks[6], (L, CMP_BLOCK, dh), 0.1),
        'nsa_ck_w1': nrm(ks[7], (L, CMP_BLOCK * dh, dh), CMP_BLOCK * dh),
        'nsa_ck_b1': small(ks[8], (L, dh), 0.02),
        'nsa_ck_w2': nrm(ks[9], (L, dh, dh), dh),
        'nsa_cv_w1': nrm(ks[10], (L, CMP_BLOCK * dh, dh), CMP_BLOCK * dh),
        'nsa_cv_b1': small(ks[11], (L, dh), 0.02),
        'nsa_cv_w2': nrm(ks[12], (L, dh, dh), dh),
        'mla_g_q': gain(ks[13], Q_LORA),
        'mla_w_uq': nrm(ks[14], (L, Q_LORA, MLA_HEADS * (QK_NOPE + QK_ROPE)), Q_LORA),
        'mla_g_kv': gain(ks[15], KV_LORA),
        'mla_w_ukv': nrm(ks[16], (L, KV_LORA, MLA_HEADS * (QK_NOPE + V_DIM)), KV_LORA),
        'w_br_nsa': nrm(ks[17], (L, NSA_WIDTH, D_MODEL), NSA_WIDTH),
        'w_br_mla': nrm(ks[18], (L, MLA_WIDTH, D_MODEL), MLA_WIDTH),
        'w_o': nrm(ks[19], (L, D_MODEL, D_MODEL), D_MODEL),
        'g_post_mix': gain(ks[20], D_MODEL),
        'g_pre_ffn': gain(ks[21], D_MODEL),
        'w_up': nrm(ks[22], (L, D_MODEL, 2 * D_FF), D_MODEL),
        'w_conv': nrm(ks[23], (L, CONV_WIDTH_2, 2 * D_FF), CONV_WIDTH_2),
        'b_conv': small(ks[24], (L, 2 * D_FF), 0.02),
        'w_down': nrm(ks[25], (L, D_FF, D_MODEL), D_FF),
        'g_post_ffn': gain(ks[26], D_MODEL),
        'w_ple': nrm(ks[27], (L, PLE_DIM, D_MODEL), PLE_DIM),
        'w_ple_gate': nrm(ks[28], (L, D_MODEL, D_MODEL), D_MODEL),
        'g_ple': gain(ks[29], D_MODEL),
    }

def second_block(x, p, positions, g_pre_mix, w_in, nsa_pos_k, nsa_pos_v, nsa_ck_w1, nsa_ck_b1, nsa_ck_w2, nsa_cv_w1, nsa_cv_b1, nsa_cv_w2, mla_g_q, mla_w_uq, mla_g_kv, mla_w_ukv, w_br_nsa, w_br_mla, w_o, g_post_mix, g_pre_ffn, w_up, w_conv, b_conv, w_down, g_post_ffn, w_ple, w_ple_gate, g_ple):
    B, T, D = x.shape
    G, R, dh = NSA_KV_GROUPS, NSA_REP, NSA_HEAD_DIM
    offsets = [int(v) for v in np.cumsum(np.array(IN_SIZES))[:-1]]
    inv_freq = ROPE_THETA ** (-jnp.arange(0, QK_ROPE, 2, dtype=jnp.float32) / QK_ROPE)
    ang = positions.astype(jnp.float32)[..., None] * inv_freq
    cos = jnp.cos(ang).astype(x.dtype)
    sin = jnp.sin(ang).astype(x.dtype)
    for i in range(DEPTH):
        h = _rmsnorm(x, g_pre_mix[i])
        proj = h @ w_in[i]
        q_n, kv_n, gate_n, c_q, c_kv, k_r, merge = jnp.split(proj, offsets, axis=-1)
        q_n = q_n.reshape(B, T, G, R, dh)
        kv_n = kv_n.reshape(B, T, 6, G, dh)
        o_nsa = _nsa_mixer(q_n, kv_n[:, :, 0], kv_n[:, :, 1], kv_n[:, :, 2], kv_n[:, :, 3], kv_n[:, :, 4], kv_n[:, :, 5], gate_n, nsa_pos_k[i], nsa_pos_v[i], nsa_ck_w1[i], nsa_ck_b1[i], nsa_ck_w2[i], nsa_cv_w1[i], nsa_cv_b1[i], nsa_cv_w2[i])
        o_mla = _mla_mixer(c_q, c_kv, k_r, cos, sin, mla_g_q[i], mla_w_uq[i], mla_g_kv[i], mla_w_ukv[i])
        gm = jax.nn.sigmoid(merge.astype(jnp.float32)).astype(x.dtype).reshape(B, T, 2, D)
        merged = gm[:, :, 0] * (o_nsa @ w_br_nsa[i]) + gm[:, :, 1] * (o_mla @ w_br_mla[i])
        x = x + _rmsnorm(merged @ w_o[i], g_post_mix[i])
        h = _rmsnorm(x, g_pre_ffn[i])
        u = _causal_dwconv(h @ w_up[i], w_conv[i], b_conv[i])
        a, v = u[..., :D_FF], u[..., D_FF:]
        x = x + _rmsnorm((jax.nn.gelu(a) * v) @ w_down[i], g_post_ffn[i])
        e = p[i] @ w_ple[i]
        gate = jax.nn.sigmoid((x @ w_ple_gate[i]).astype(jnp.float32)).astype(x.dtype)
        x = x + _rmsnorm(e * gate, g_ple[i])
    return x


def setup_inputs(seed=0):
    out = dict(first_inputs(seed))
    for name, value in second_inputs(seed + 1).items():
        if name != "x":
            out[name + "_2"] = value
    return out


def reference(
    x, mem, norm_mix, w_in, conv_w, dn_conv_w, dn_a_log, dn_dt_bias, dn_norm, w_out, norm_x,
    norm_mem, w_xq, w_xkv, w_xo, norm_ffn, w_pq, peer_keys, expert_u, expert_v, norm_final, p_2,
    positions_2, g_pre_mix_2, w_in_2, nsa_pos_k_2, nsa_pos_v_2, nsa_ck_w1_2, nsa_ck_b1_2,
    nsa_ck_w2_2, nsa_cv_w1_2, nsa_cv_b1_2, nsa_cv_w2_2, mla_g_q_2, mla_w_uq_2, mla_g_kv_2,
    mla_w_ukv_2, w_br_nsa_2, w_br_mla_2, w_o_2, g_post_mix_2, g_pre_ffn_2, w_up_2, w_conv_2,
    b_conv_2, w_down_2, g_post_ffn_2, w_ple_2, w_ple_gate_2, g_ple_2,
):
    x = first_block(
        x, mem, norm_mix, w_in, conv_w, dn_conv_w, dn_a_log, dn_dt_bias, dn_norm, w_out, norm_x,
        norm_mem, w_xq, w_xkv, w_xo, norm_ffn, w_pq, peer_keys, expert_u, expert_v, norm_final,
    )
    return second_block(
        x, p_2, positions_2, g_pre_mix_2, w_in_2, nsa_pos_k_2, nsa_pos_v_2, nsa_ck_w1_2,
        nsa_ck_b1_2, nsa_ck_w2_2, nsa_cv_w1_2, nsa_cv_b1_2, nsa_cv_w2_2, mla_g_q_2, mla_w_uq_2,
        mla_g_kv_2, mla_w_ukv_2, w_br_nsa_2, w_br_mla_2, w_o_2, g_post_mix_2, g_pre_ffn_2,
        w_up_2, w_conv_2, b_conv_2, w_down_2, g_post_ffn_2, w_ple_2, w_ple_gate_2, g_ple_2,
    )


_drawn_inputs = setup_inputs


def setup_inputs(seed=0):
    import zlib

    import numpy as np

    out = dict(_drawn_inputs(seed))
    spreads = {}
    factors = {'dn_norm': 4.127,
     'norm_x': 8.0,
     'norm_mem': 7.808,
     'norm_ffn': 8.852,
     'nsa_pos_k_2': 62.616,
     'nsa_ck_b1_2': 200.0,
     'nsa_cv_b1_2': 30.441,
     'mla_g_q_2': 4.081,
     'mla_g_kv_2': 3.154,
     'b_conv_2': 3.848,
     'nsa_pos_v_2': 6.789,
     'nsa_ck_w1_2': 3.907,
     'nsa_ck_w2_2': 3.978}
    for name, (base, spread) in spreads.items():
        noise = np.random.default_rng([zlib.crc32(name.encode()), seed]).standard_normal(out[name].shape)
        drawn = base * np.exp(spread * noise) if base else spread * noise
        out[name] = jnp.asarray(drawn.astype(out[name].dtype))
    for name, factor in factors.items():
        out[name] = (out[name] * factor).astype(out[name].dtype)
    return out
```

```python
from contextlib import ExitStack

import numpy as np

import concourse.bass as bass
from concourse import mybir

F32 = mybir.dt.float32
F32R = mybir.dt.float32r
I32 = mybir.dt.int32
U32 = mybir.dt.uint32
ACT = mybir.ActivationFunctionType
ALU = mybir.AluOpType
AXX = mybir.AxisListType.X

P = 128
D = 1024
T = 512
TB = T // P
KC = D // P
EPS = 1e-6

CW = 512
CONV_K = 3
DN_H = 4
DN_CONV_K = 4
CHUNK = 64
MEM = 256
X_H = 4
PH = 8
NKEY = 128
TOPK = 16
SEL = PH * TOPK
NH = 8
G = 2
DH = 64
CMP_L = 32
CMP_S = 16
NCMP = (T - CMP_L) // CMP_S + 1
QL = 256
NOPE = 64
ROPE = 32
DFF = 2816
FC = DFF // P
PLE = 256
NEG = -1e30

SLOTS = 3
SLOT_W = 4096

VEC = [
    ("ident", P), ("ones", P), ("eps", 1), ("norm_mix", KC), ("norm_mem", KC), ("norm_x", KC),
    ("conv_w", 4 * CONV_K), ("dn_conv_w", 12 * DN_CONV_K), ("dn_norm", 1), ("a_log", 1), ("dt_bias", 1),
    ("w_ba", KC * 8), ("iota16", TOPK), ("pre_mix", KC), ("pre_ffn", KC), ("q_scale", 4),
    ("ck_b1", 1), ("cv_b1", 1), ("pos_k", CMP_L), ("pos_v", CMP_L), ("ck_w2", P), ("cv_w2", P),
    ("g_q", 2), ("g_kv", 1), ("inv_freq", 1), ("rot", ROPE), ("up_conv", 2 * FC * 3), ("up_b", 2 * FC),
]
GDN = [("causal", P), ("level", 6 * P), ("pick", DN_H * P), ("restart", T)]
ATT = [("negdist", T), ("causal_neg", T), ("cmp_dist", TB * NCMP), ("cmp_mask", TB * NCMP)]


def offsets(pack):
    at, out = 0, {}
    for name, width in pack:
        out[name] = (at, width)
        at += width
    return out, at


VEC_AT, VEC_W = offsets(VEC)
GDN_AT, GDN_W = offsets(GDN)
ATT_AT, ATT_W = offsets(ATT)

RAW_TILES = ("peer_keys", "ck_w1", "cv_w1", "w_uq", "w_ukv", "w_br_nsa", "w_br_mla", "w_ple0", "w_ple1")


def by_columns(name, n):
    return [(f"{name}{c}", KC * 256) for c in range(n)]


def by_rows(name, rows=(4, 4)):
    return [(f"{name}{n}_{k}", r * 512) for n in range(2) for k, r in enumerate(rows)]


DOWN_ROWS = (4, 4, 4, 4, 4, 2)
WEIGHT_TILES = (
    by_columns("w_in", 14) + by_rows("w_out") + by_columns("w_xk", 4) + by_rows("w_xv")
    + by_columns("w_xq", 4) + by_rows("w_xo") + by_columns("w_pq", 4) + [("peer_keys", PH * NKEY)]
    + by_columns("w2_q", 2) + by_columns("w2_kv", 2) + [("w2_kw", KC * 128), ("w2_vwg", KC * 152)]
    + [("w2_cq_0", 4 * 384), ("w2_cq_1", 4 * 384), ("w2_kr", KC * 96)]
    + [("ck_w1", CMP_L * P), ("cv_w1", CMP_L * P)] + by_columns("w2_merge", 8)
    + [("w_uq", 2 * 768), ("w_ukv", 1024)]
    + [("w_br_nsa", 4 * D), ("w_br_mla", 4 * D)] + by_rows("w_o")
    + by_columns("w_up", 22) + by_rows("w_down", DOWN_ROWS)
    + by_rows("w_pg")[:2] + [("w_ple0", D)] + by_rows("w_pg")[2:] + [("w_ple1", D)]
)
TILE_NO = {name: n for n, (name, _) in enumerate(WEIGHT_TILES)}
TILE_AT = {}
_at = 0
for _name, _w in WEIGHT_TILES:
    TILE_AT[_name] = _at
    _at += P * _w
STREAM = _at
SPLIT_NO = {name: n for n, name in enumerate(n for n, _ in WEIGHT_TILES if n not in RAW_TILES)}
SPLIT_STAGES = [[n for n in SPLIT_NO if n.startswith(stage)] for stage in
                (("w_in", "w_out"), ("w_x",), ("w_pq",), ("w2_",), ("w_o0", "w_o1"), ("w_up", "w_down"), ("w_pg",))]
ACT_HIGHS = ["w_xk3", "w_xv0_0", "w_xv0_1", "w_xv1_0", "w_xv1_1",
             "w2_kv1", "w2_kw", "w2_vwg", "w2_cq_0", "w2_cq_1", "w2_kr"]
FFN_TILES = [n for n in SPLIT_NO if n.startswith(("w_up", "w_down"))]
ACT_HIGHS += FFN_TILES[SLOTS:]
LEVELS = [1, 2, 4, 8, 16, 32]
PEER_BODY = 2
GROUP = 8
TOPK_STEPS = 29
SCORES_AHEAD = 3
AHEAD = 2


def build(nc, io):
    with ExitStack() as ctx:
        def sb(name, shape, dt=F32):
            return ctx.enter_context(nc.sbuf_tensor(name, shape, dt))

        sems = {}

        def S(name):
            if name not in sems:
                sems[name] = ctx.enter_context(nc.semaphore(name))
            return sems[name]

        AREA = 31264
        with nc.sbuf_tensor("ring", [P, SLOTS, SLOT_W], F32) as ring, nc.sbuf_tensor("XT", [P, KC, T], F32) as XT, \
                nc.sbuf_tensor("area", [P, AREA], F32) as area:
            pass
        area_cuts = (0, 12288, 23552, AREA)
        ring_rounded = sb("ring_rounded", [P, SLOTS, SLOT_W], F32R)
        XT_rounded = sb("XT_rounded", [P, KC, T], F32R)
        area_rounded = [sb(f"area_rounded{n}", [P, area_cuts[n + 1] - area_cuts[n]], F32R) for n in range(3)]
        H = sb("H", [P, TB, D])
        vec = sb("vec", [P, VEC_W])
        WBA = [sb("w_ba_high", [P, KC * 8], F32R), sb("w_ba_low", [P, KC * 8], F32R)]
        stats = sb("stats", [P, 320])

        def rounded(piece):
            name, ap = piece.tensor.name, list(piece.ap)
            if name != "area":
                return bass.AP(tensor=ring_rounded if name == "ring" else XT_rounded, offset=piece.offset, ap=ap)
            end = piece.offset + sum(step * (count - 1) for step, count in ap[1:])
            n = sum(piece.offset >= cut for cut in area_cuts) - 1
            assert end < area_cuts[n + 1], (piece.offset, end)
            width = area_cuts[n + 1] - area_cuts[n]
            return bass.AP(tensor=area_rounded[n], offset=piece.offset - area_cuts[n], ap=[[width, P]] + ap[1:])

        psum = [ctx.enter_context(nc.psum_tensor(f"psum{b}", [P, 512], F32)) for b in range(8)]
        psum_full = [S(f"psum_full{b}") for b in range(8)]
        psum_read = [S(f"psum_read{b}") for b in range(8)]

        def V(name, a=0, b=None):
            at, width = VEC_AT[name]
            return vec[:, at + a:at + (width if b is None else b)]

        def region(at, *shape):
            n = 1
            for s in shape:
                n *= s
            assert at + n <= AREA, (at, shape)
            flat = area[:, at:at + n]
            if len(shape) == 1:
                return flat
            names = "abcd"[:len(shape)]
            kw = {names[j]: shape[j] for j in range(len(shape))}
            return flat.rearrange(f"p ({' '.join(names)}) -> p {' '.join(names)}", **kw)

        ident = V("ident")
        ones = V("ones")
        eps = V("eps")

        def stat(n, w=TB):
            return stats[:, 8 * n:8 * n + w]

        bank_of = {}
        order = [0]
        tile_free = {}

        def take(pe, name):
            n = order[0]
            order[0] += 1
            b, use = n % 8, n // 8
            assert name not in bank_of, name
            bank_of[name] = (b, use)
            if use:
                pe.wait_ge(psum_read[b], use)
            return psum[b]

        def fin(ins, name):
            ins.then_inc(psum_full[bank_of[name][0]], 1)

        def full(eng, name):
            b, use = bank_of[name]
            eng.wait_ge(psum_full[b], use + 1)
            return psum[b]

        def read(ins, name):
            ins.then_inc(psum_read[bank_of[name][0]], 1)

        def read_out(eng, name):
            b, use = bank_of[name]
            eng.wait_ge(psum_read[b], use + 1)

        def psum_uses(b):
            return (order[0] - b + 7) // 8

        def tile_in(pe, name):
            n = TILE_NO[name]
            pe.wait_ge(S(f"weights_landed{n % SLOTS}"), 16 * (n // SLOTS + 1))
            return ring[:, n % SLOTS, :]

        def tile_done(name, product):
            b, use = bank_of[product]
            tile_free[name] = (psum_full[b], use + 1)

        def pair(high, low):
            return rounded(high), rounded(low)

        YT = region(0, 8, T)
        QKV = region(4096, 12, T)
        ZT = region(10240, 4, T)
        gdn = region(12288, GDN_W)
        SS = region(12288 + GDN_AT["pick"][0], DN_H, P)
        states = [SS, region(12288 + GDN_AT["level"][0], DN_H, P)]
        VN = region(12288 + GDN_AT["restart"][0], DN_H, P)
        o = 12288 + GDN_W
        GB = region(o, DN_H, T)
        EGB = region(o + 2048, DN_H, T)
        BB = region(o + 4096, DN_H, T)
        CM = region(o, TB, DN_H * P)
        XM = region(o + 4096, TB, DN_H * P)
        ROWT = region(o + 4096, 4, T)
        o += 6144
        KB = region(o, TB, DN_H, P)
        KD = region(o + 2048, TB, DN_H, P)
        VB = region(o + 4096, TB, DN_H, P)
        LSQ = region(o, 2, T)
        LRT = region(o + 1024, 2, T)
        ROWS = region(o + 2048, 5, T)
        CONVT = region(o + 5120, 2, T)
        o += 6144
        BT = YT[:, 4:8, :]
        DT = BT.rearrange("p a (h i) -> p a h i", h=DN_H)
        CT = region(o, 4, T)
        AT = region(o, TB, DN_H, P)
        UU = DT
        WT = AT
        XN1 = region(4096, TB, D)
        TM = XT[:, 0:4, :].rearrange("p a (h i) -> p a h i", h=DN_H)
        TT = XT[:, 4:8, :].rearrange("p a (h i) -> p a h i", h=DN_H)
        OT = QKV[:, 4:8, :]
        IN = region(o + 2048, TB, DN_H, P)
        TOK = stats[:, 96:160]

        XL1 = region(14208, KC, T)

        def XT1(k):
            return pair(XT[:, k, :], XL1[:, k, :])

        def YH(k):
            return region(24448 if k < 4 else 14208, 4, T)[:, k % 4, :]

        def gd(name, a=0, b=None):
            at, width = GDN_AT[name]
            return gdn[:, at + a:at + (width if b is None else b)]

        MEMX = region(18304, 2, D)
        MEMN = XT[:, 0:4, :].rearrange("p (b c) t -> p b (c t)", b=2)
        MT = region(4096, KC, MEM)
        MK = region(6144, KC, MEM)
        MV = region(8192, 2, D)
        XNX = region(10240, TB, D)
        XQ = region(14336, KC, T)
        XP = [region(18432, 2, MEM), region(18944, 2, MEM), region(29696, 2, MEM), region(30208, 2, MEM)]
        XPT = region(19456, X_H * 2, T)
        XO = region(23552, KC, T)

        MTL = region(27648, KC, MEM)
        XL2 = region(0, KC, T)
        XOL = region(10240, KC, T)

        PX = region(0, TB, D)
        SC = region(4096, 2, TB * PH * NKEY)
        UR = region(12288, GROUP, D)
        VR = region(20480, GROUP, D)
        PQ = region(12288, KC, T)
        XL3 = region(16384, KC, T)
        GAIN = region(28672, D)
        FGAIN = XT[:, 4:6, :].rearrange("p a b -> p (a b)")
        FSQ = region(4096, TB, D)
        IDX = region(28672, TB * SEL).bitcast(U32)
        GATE = region(29184, TB * SEL)
        DIAG = region(29696, GROUP, P)
        small = XT[:].rearrange("p a b -> p (a b)")

        def tiny(at, *shape):
            n = int(np.prod(shape))
            flat = small[:, at:at + n]
            if len(shape) == 1:
                return flat
            names = "abcd"[:len(shape)]
            kw = {names[j]: shape[j] for j in range(len(shape))}
            return flat.rearrange(f"p ({' '.join(names)}) -> p {' '.join(names)}", **kw)

        TS = tiny(0, 2, NKEY)
        TS2 = tiny(256, 2, NKEY)
        TV = tiny(512, 2, TOPK)
        TI = tiny(544, 2, TOPK).bitcast(U32)
        TIF = tiny(576, 2, TOPK)
        CAND = tiny(608, TOPK, TOPK)
        CAND2 = tiny(864, TOPK, TOPK)
        BEST = tiny(1120, TOPK)
        POS = tiny(1136, TOPK).bitcast(U32)
        PAB = tiny(1152, 2, TOPK).bitcast(U32)
        PABF = tiny(1184, 2, TOPK)
        EQ = tiny(1216, 2, TOPK, TOPK)
        IJ = tiny(1728, 2, TOPK)
        IDF = tiny(1760, TOPK)
        NB = tiny(1776, 1)
        GSUM = tiny(1777, 1)
        GINV = tiny(1778, 1)
        GE = tiny(1792, TOPK)
        DOTS = tiny(1808, 2, GROUP)
        ACTS = tiny(1824, 2, GROUP)
        W8 = tiny(1840, 2, GROUP)
        IG = tiny(1856, 2, GROUP).bitcast(U32)

        att = region(0, ATT_W)
        o = ATT_W
        GA = region(o, D)
        GT = region(o + D, TB, 3 * NH)
        SB = region(o + D + 96, 2, T)
        o += D + 96 + 2 * T
        GM = region(o, 16, T)
        XN2 = region(o, TB, D)
        FFN_SQ = region(o + 4096, TB, D)

        def unit_rows(u):
            return SB[:, u % 4, :] if u % 4 < 2 else XT[:, u % 4 - 2, :]

        o += 16 * T
        PT = region(o, 3, TB, T)
        PB = region(o, 2, CMP_L, NCMP)
        SQ2 = region(o, TB, 384)
        RT = XT[:, 2:4, :]
        o += 3 * TB * T
        XL4 = region(o - 2 * TB * T, KC, T)
        MGH = region(o - 2 * TB * T, KC, T)
        ON = region(o, 4, T)
        o += 4 * T
        QN = region(o, 4, T)
        KX = region(o + 2048, 4, T)
        VX = region(o + 4096, 2, TB, P)
        PC = region(o + 5120, 2, NH, 32)
        PCT = region(o + 5632, 2, T)
        HID = region(o + 6656, 2, 32)
        KCMP = region(o + 6720, 32)
        VC4 = region(o + 6752, P)
        QM = region(o, NH, T)
        KM = region(o + 4096, NH, T)
        OM = region(o + 8192, 4, T)
        KR = region(o + 8192, T)
        CQ = region(o + 8704, TB, 384)
        COS = region(o + 10240, T)
        SIN = region(o + 10752, T)
        ANG = [SIN, region(o + 6912, T), region(o + 7424, T), COS]
        VM = XT[:, 4:8, :]
        MG = region(19968, KC, T)
        YB = region(24064, TB, D)

        def at_(name, a=0, b=None):
            at, width = ATT_AT[name]
            return att[:, at + a:at + (width if b is None else b)]

        FX = region(0, TB, D)
        AC = region(4096, 2, 4, T)
        MF = region(8192, FC, T)
        YF = region(8192 + FC * T, TB, D)
        XL5 = region(8192 + FC * T, KC, T)
        GF = region(4096, D)
        GP = region(5120, D)
        PI = region(6144, TB, PLE)

        def MFH(k):
            return region(0, 8, T)[:, k, :] if k < 8 else region(12288 + FC * T, 14, T)[:, k - 8, :]

        PLT = region(8192, 2, T)
        SG = region(9216, 2, T)
        YP = region(10240, TB, D)
        FQ = region(14336, TB, D)

        block = ctx.enter_context(nc.Block())

        STAGE_ENGINES = 3

        def stage_end(eng, n):
            eng.drain().then_inc(S("stage_end"), 1)
            eng.wait_ge(S("stage_end"), STAGE_ENGINES * n)

        norm_blocks = [("mix", TB), ("mem", 2), ("x", TB), ("peer", TB), ("final", TB), ("pre", TB), ("cq", TB),
                       ("ckv", TB), ("post", TB), ("ffn", TB), ("down", TB), ("ple", TB)]
        norm_no = {n: j for j, (n, _) in enumerate(norm_blocks)}
        norm_sums = {n: sum(m for _, m in norm_blocks[:j]) for j, (n, _) in enumerate(norm_blocks)}

        def act_norm(act, name, src, dst, st, ntb=TB, ready=None):
            for b in range(ntb):
                if ready is not None:
                    ready(act, b)
                act.activation(dst(b), src(b), ACT.Square, accum_out=stat(st, ntb)[:, b:b + 1])\
                   .then_inc(S("norm_sumsq"), 1)
            act.wait_ge(S("norm_meansq"), norm_no[name] + 1)
            act.activation(stat(st + 1, ntb), stat(st, ntb), ACT.Sqrt).then_inc(S("norm_root"), 1)

        def dve_mean(dve, name, st, width, ntb):
            dve.wait_ge(S("norm_sumsq"), norm_sums[name] + ntb)
            dve.tensor_scalar(stat(st, ntb), stat(st, ntb), 1.0 / width, EPS, ALU.mult, ALU.add)\
               .then_inc(S("norm_meansq"), 1)

        def dve_scale(dve, name, st, ntb):
            dve.wait_ge(S("norm_root"), norm_no[name] + 1)
            dve.reciprocal(stat(st + 2, ntb), stat(st + 1, ntb)).then_inc(S("norm_inv"), 1)
            dve.wait_ge(S("norm_inv"), norm_no[name] + 1)
            return stat(st + 2, ntb)

        def dve_norm_scale(dve, name, st, width, ntb=TB):
            dve_mean(dve, name, st, width, ntb)
            return dve_scale(dve, name, st, ntb)

        def pe_transposes(pe, name, src, ready, ntb=TB, chunks=KC):
            ready()
            for c in range(chunks):
                ps = take(pe, (name, c))
                for b in range(ntb):
                    ins = pe.transpose(ps[:, b * P:(b + 1) * P], src(b, c), ident)
                fin(ins, (name, c))

        def mm3(pe, out, lhs, rhs, start, stop):
            pe.matmul(out, lhs[1], rhs[0], start=start, stop=False)
            pe.matmul(out, lhs[0], rhs[1], start=False, stop=False)
            return pe.matmul(out, lhs[0], rhs[0], start=False, stop=stop)

        def cut(parts, a, b):
            return parts[0][:, a:b], parts[1][:, a:b]

        def split_in(pe, name):
            pe.wait_ge(S("weights_split"), SPLIT_NO[name] + 1)
            slot = ring[:, TILE_NO[name] % SLOTS, :]
            return pair(slot[:, SLOT_W // 2:], slot[:, 0:SLOT_W // 2])

        def tile_parts(name):
            n, w = TILE_NO[name], dict(WEIGHT_TILES)[name]
            raw = ring[:, n % SLOTS, 0:w]
            high, low = pair(ring[:, n % SLOTS, SLOT_W // 2:SLOT_W // 2 + w], raw)
            return n, w, raw, high, low

        pool_highs = [0]

        def split_weights(pool, names):
            for name in names:
                n, w, raw, high, low = tile_parts(name)
                if name in ACT_HIGHS:
                    pool.wait_ge(S("tile_high"), ACT_HIGHS.index(name) + 1)
                else:
                    pool.wait_ge(S(f"weights_landed{n % SLOTS}"), 16 * (n // SLOTS + 1))
                    pool.tensor_tensor(high, raw, V("ones", 0, 1).to_broadcast([P, w]), ALU.mult)\
                        .then_inc(S("high_made"), 1)
                    pool_highs[0] += 1
                    pool.wait_ge(S("high_made"), pool_highs[0])
                pool.tensor_tensor(low, raw, high.bitcast(F32), ALU.subtract).then_inc(S("weights_split"), 1)

        def act_tile_high(act, name):
            n, w, raw, high, low = tile_parts(name)
            act.wait_ge(S(f"weights_landed{n % SLOTS}"), 16 * (n // SLOTS + 1))
            act.activation(high, raw, ACT.Copy).then_inc(S("tile_high"), 1)

        high_order = ["mixT", "memT", "xT", "xo", "pT", "mT", "fT", "hT"]

        def act_high(act, name, product, dst, c, scale=1.0):
            ps = full(act, product)
            act.activation(rounded(dst), ps[:, 0:dst.shape[-1]], ACT.Copy, scale=scale)\
               .then_inc(S("act_high"), 1)

        def dve_low(dve, name, product, high, low, c, scale=1.0):
            dve.wait_ge(S("act_high"), KC * high_order.index(name) + c + 1)
            ps = full(dve, product)
            read(dve.scalar_tensor_tensor(out=rounded(low), in0=ps[:, 0:low.shape[-1]], scalar=scale,
                                          in1=rounded(high).bitcast(F32),
                                          op0=ALU.mult, op1=ALU.subtract), product)

        def pe_feature(pe, name, first, tile, ncols, cols, rhs, n):
            for m, c0 in enumerate(cols):
                ps = take(pe, (name, first + m))
                for k in range(KC):
                    at = k * ncols + c0
                    ins = mm3(pe, ps[:, 0:n], cut(tile, at, at + P), rhs(k), k == 0, k == KC - 1)
                fin(ins, (name, first + m))

        def pe_feature_tiles(pe, name, tiles, rhs, n=T):
            for t, tile in enumerate(tiles):
                w = split_in(pe, tile)
                pe_feature(pe, (name, t // 2), 2 * (t % 2), w, 256, (0, P), rhs, n)
                tile_done(tile, ((name, t // 2), 2 * (t % 2) + 1))

        def pe_token(pe, name, tile, ncols, c0, n, lhs, ntb=TB):
            for b in range(ntb):
                ps = take(pe, (name, b))
                for k in range(KC):
                    at = k * ncols + c0
                    ins = mm3(pe, ps[:, 0:n], lhs(k, b), cut(tile, at, at + n), k == 0, k == KC - 1)
                fin(ins, (name, b))

        parts_used = [0]

        def pe_token_rows(pe, names, tiles, rows, n, lhs):
            banks = [take(pe, name) for name in names]
            k0 = 0
            for t, tile in enumerate(tiles):
                w = split_in(pe, tile)
                last = t == len(tiles) - 1
                for b, name in enumerate(names):
                    for k in range(rows[t]):
                        ins = mm3(pe, banks[b][:, 0:n], lhs(k0 + k, b), cut(w, k * n, (k + 1) * n),
                                  t == 0 and k == 0, last and k == rows[t] - 1)
                    if last:
                        fin(ins, name)
                k0 += rows[t]
                if not last:
                    ins.then_inc(S("rows_used"), 1)
                    parts_used[0] += 1
                    tile_free[tile] = (S("rows_used"), parts_used[0])
            tile_done(tiles[-1], names[-1])

        @block.tensor
        def _(pe):
            pe.wait_ge(S("vec_landed"), 16)
            pe_transposes(pe, "mixT", lambda b, c: XN1[:, b, c * P:(c + 1) * P],
                          lambda: pe.wait_ge(S("mix_scaled"), TB))
            for c in range(KC):
                read_out(pe, ("mixT", c))
            pe.wait_ge(S("ba_split"), 2)
            for n, name in enumerate(("beta", "a")):
                ps = take(pe, name)
                for k in range(KC):
                    ins = mm3(pe, ps[0:4, :], cut(WBA, 8 * k + 4 * n, 8 * k + 4 * n + 4), XT1(k), k == 0, k == KC - 1)
                fin(ins, name)
            pe_feature_tiles(pe, "proj", [f"w_in{n}" for n in range(14)], XT1)
            for j in range(8):
                pe.wait_ge(S("qk_squared"), j + 1)
                ps = take(pe, ("l2", j))
                fin(pe.matmul(ps[:], ones, LSQ[:, j % 2, :], start=True, stop=True), ("l2", j))
            pe.wait_ge(S("rows_done"), 1)
            pe.wait_ge(S("gdn_landed"), 16)
            for r in range(3):
                for h in range(DN_H):
                    ps = take(pe, ("rowb", r, h))
                    fin(pe.matmul(ps[:], gd("pick", h * P, (h + 1) * P)[0:4, :], ROWS[0:4, r, :],
                                  start=True, stop=True), ("rowb", r, h))
            ps = take(pe, "tok")
            for j, r in enumerate((0, 2, 3, 4)):
                for b in range(TB):
                    ins = pe.transpose(ps[:, 16 * j + 4 * b:16 * j + 4 * b + 4],
                                       ROWS[0:4, r, b * P:(b + 1) * P], ident[0:4, 0:4])
            fin(ins, "tok")
            pe.wait_ge(S("qk_normed"), 8)
            for b in range(TB):
                at = slice(b * P, (b + 1) * P)
                for name, c in (("kt", 4), ("vt", 8)):
                    ps = take(pe, (name, b))
                    if name == "vt":
                        pe.wait_ge(S("v_done"), 4)
                    for h in range(DN_H):
                        ins = pe.transpose(ps[:, h * P:(h + 1) * P], QKV[:, c + h, at], ident)
                    fin(ins, (name, b))
                for name, c in (("kk", 4), ("qk", 0)):
                    ps = take(pe, (name, b))
                    for h in range(DN_H):
                        ins = pe.matmul(ps[:, h * P:(h + 1) * P], QKV[:, 4 + h, at], QKV[:, c + h, at],
                                        start=True, stop=True)
                    fin(ins, (name, b))
            for b in range(TB):
                pe.wait_ge(S("tt_start"), b + 1)
                ps = take(pe, ("t0", b))
                for h in range(DN_H):
                    ins = pe.transpose(ps[:, h * P:(h + 1) * P], TT[:, b, h, :], ident)
                fin(ins, ("t0", b))
            for lv in range(1, 6):
                for b in range(TB):
                    pe.wait_ge(S("c_masked"), (lv - 1) * TB + b + 1)
                    if lv == 1:
                        read_out(pe, ("t0", b))
                    else:
                        read_out(pe, ("dt", lv - 1, b))
                    ps = take(pe, ("x", lv, b))
                    for h in range(DN_H):
                        ins = pe.matmul(ps[:, h * P:(h + 1) * P], CM[:, b, h * P:(h + 1) * P], TM[:, b, h, :],
                                        start=True, stop=True)
                    fin(ins, ("x", lv, b))
                for b in range(TB):
                    read_out(pe, ("x", lv, b))
                    if lv > 1:
                        read_out(pe, ("dtt", lv - 1, b))
                    if lv < 5:
                        ps = take(pe, ("dt", lv, b))
                        for h in range(DN_H):
                            ins = pe.matmul(ps[:, h * P:(h + 1) * P], TT[:, b, h, :], XM[:, b, h * P:(h + 1) * P],
                                            start=True, stop=True)
                        fin(ins, ("dt", lv, b))
                    ps = take(pe, ("dtt", lv, b))
                    for h in range(DN_H):
                        ins = pe.matmul(ps[:, h * P:(h + 1) * P], XM[:, b, h * P:(h + 1) * P], TT[:, b, h, :],
                                        start=True, stop=True)
                    fin(ins, ("dtt", lv, b))
            for b in range(TB):
                read_out(pe, ("dtt", 5, b))
                ps = take(pe, ("u", b))
                for h in range(DN_H):
                    ins = pe.matmul(ps[:, h * P:(h + 1) * P], TT[:, b, h, :], VB[:, b, h, :], start=True, stop=True)
                fin(ins, ("u", b))
                ps = take(pe, ("w", b))
                for h in range(DN_H):
                    ins = pe.matmul(ps[:, h * P:(h + 1) * P], KB[:, b, h, :], TT[:, b, h, :], start=True, stop=True)
                fin(ins, ("w", b))
            pe.wait_ge(S("qdec_done"), 4)
            pe.wait_ge(S("state_zero"), 1)
            for c in range(8):
                b, r = c // 2, slice(CHUNK * (c % 2), CHUNK * (c % 2) + CHUNK)
                read_out(pe, ("w", b))
                state = states[c % 2]
                ps = take(pe, ("ws", c))
                for h in range(DN_H):
                    if c:
                        pe.wait_ge(S("state_done"), 4 * (c - 1) + h + 1)
                    ins = pe.matmul(ps[r, h * P:(h + 1) * P], WT[:, b, h, r], state[:, h, :], start=True, stop=True)
                fin(ins, ("ws", c))
                po = take(pe, ("o", c))
                for h in range(DN_H):
                    pe.matmul(po[:, h * CHUNK:(h + 1) * CHUNK], state[:, h, :], QKV[:, h, c * CHUNK:(c + 1) * CHUNK],
                              start=(h == 0), stop=False)
                read_out(pe, ("ws", c))
                ps = take(pe, ("kv", c))
                for h in range(DN_H):
                    ins = pe.matmul(ps[:, h * P:(h + 1) * P], KD[r, b, h, :], VN[r, h, :], start=True, stop=True)
                fin(ins, ("kv", c))
                for h in range(DN_H):
                    ins = pe.matmul(po[:, h * CHUNK:(h + 1) * CHUNK], VN[r, h, :], IN[r, b, h, r],
                                    start=False, stop=(h == DN_H - 1))
                fin(ins, ("o", c))
            for h in range(DN_H):
                pe.wait_ge(S("o_squared"), h + 1)
                ps = take(pe, ("on", h))
                fin(pe.matmul(ps[:], ones, LSQ[:, h % 2, :], start=True, stop=True), ("on", h))
            pe_transposes(pe, "memT", lambda b, c: MEMN[:, b, c * P:(c + 1) * P],
                          lambda: pe.wait_ge(S("mem_scaled"), 2), ntb=2)
            pe.wait_ge(S("y_low"), 8)
            for n in range(2):
                pe_token_rows(pe, [(("mo", n), b) for b in range(TB)], [f"w_out{n}_0", f"w_out{n}_1"], (4, 4), 512,
                              lambda k, b: pair(YH(k)[:, b * P:(b + 1) * P], YT[:, k, b * P:(b + 1) * P]))
            stage_end(pe, 1)
            for c in range(KC):
                read_out(pe, ("memT", c))
            pe_feature_tiles(pe, "xk", [f"w_xk{n}" for n in range(4)], lambda k: pair(MT[:, k, :], MTL[:, k, :]), MEM)
            for n in range(2):
                pe_token_rows(pe, [(("xv", n), b) for b in range(2)], [f"w_xv{n}_0", f"w_xv{n}_1"], (4, 4), 512,
                              lambda k, b: pair(MT[:, k, b * P:(b + 1) * P], MTL[:, k, b * P:(b + 1) * P]))
            pe_transposes(pe, "xT", lambda b, c: XNX[:, b, c * P:(c + 1) * P],
                          lambda: pe.wait_ge(S("x_scaled"), TB))
            for c in range(KC):
                read_out(pe, ("xT", c))
            pe_feature_tiles(pe, "xq", [f"w_xq{n}" for n in range(4)], lambda k: pair(XT[:, k, :], XL2[:, k, :]))
            for n in range(2):
                for m in range(4):
                    read_out(pe, (("xk", n), m))
                    read_out(pe, (("xq", n), m))

            def x_scores(u):
                hp, b = divmod(u, TB)
                ps = take(pe, ("xs", u))
                for h2 in range(2):
                    for dc in range(2):
                        c = 2 * (2 * hp + h2) + dc
                        ins = pe.matmul(ps[:, h2 * MEM:(h2 + 1) * MEM], XQ[:, c, b * P:(b + 1) * P], MK[:, c, :],
                                        start=(dc == 0), stop=(dc == 1))
                fin(ins, ("xs", u))

            for u in range(SCORES_AHEAD):
                x_scores(u)
            for u in range(8):
                if u + SCORES_AHEAD < 8:
                    x_scores(u + SCORES_AHEAD)
                pe.wait_ge(S("xp_ready"), 2 * (u + 1))
                ps = take(pe, ("xpT", u))
                for h2 in range(2):
                    for mc in range(2):
                        ins = pe.transpose(ps[:, (2 * h2 + mc) * P:(2 * h2 + mc + 1) * P],
                                           XP[u % 4][:, h2, mc * P:(mc + 1) * P], ident)
                fin(ins, ("xpT", u))
            for n in range(2):
                for b in range(2):
                    read_out(pe, (("xv", n), b))
            for u in range(8):
                read_out(pe, ("xpT", u))
            for h in range(X_H):
                for dc in range(2):
                    ps = take(pe, ("xo", h, dc))
                    for mc in range(2):
                        ins = pe.matmul(ps[:], MV[:, mc, h * 256 + dc * P:h * 256 + (dc + 1) * P],
                                        XPT[:, 2 * h + mc, :], start=(mc == 0), stop=(mc == 1))
                    fin(ins, ("xo", h, dc))
            for h in range(X_H):
                for dc in range(2):
                    read_out(pe, ("xo", h, dc))
            for n in range(2):
                pe_token_rows(pe, [(("xout", n), b) for b in range(TB)], [f"w_xo{n}_0", f"w_xo{n}_1"], (4, 4), 512,
                              lambda k, b: pair(XO[:, k, b * P:(b + 1) * P], XOL[:, k, b * P:(b + 1) * P]))
            stage_end(pe, 2)
            pe_transposes(pe, "pT", lambda b, c: PX[:, b, c * P:(c + 1) * P],
                          lambda: pe.wait_ge(S("peer_scaled"), TB))
            for c in range(KC):
                read_out(pe, ("pT", c))
            pe_feature_tiles(pe, "pq", [f"w_pq{n}" for n in range(4)], lambda k: pair(XT[:, k, :], XL3[:, k, :]))
            for n in range(2):
                for m in range(4):
                    read_out(pe, (("pq", n), m))
            w = tile_in(pe, "peer_keys")
            for b in range(TB):
                for hp in range(4):
                    ps = take(pe, ("ps", b, hp))
                    for j in range(4):
                        h, half = 4 * (hp // 2) + j, slice(64 * (hp % 2), 64 * (hp % 2) + 64)
                        ins = pe.matmul(ps[:, j * P:(j + 1) * P], PQ[half, h, b * P:(b + 1) * P],
                                        w[half, h * NKEY:(h + 1) * NKEY], start=True, stop=True)
                    fin(ins, ("ps", b, hp))
            tile_done("peer_keys", ("ps", TB - 1, 3))
            for b in range(8):
                if psum_uses(b):
                    pe.wait_ge(psum_read[b], psum_uses(b))

            def peer_pe(i):
                for par in range(2):
                    g = 2 * i + par
                    pe.wait_ge(S("peer_added"), 4 * i + 1)
                    for s in range(GROUP):
                        pe.wait_ge(S("diag_made"), GROUP * g + (s + 1))
                        pe.wait_ge(S(f"v_landed{s}"), 16 * g + 16)
                        for k in range(2):
                            ins = pe.matmul(psum[2 * par + k][:], DIAG[:, s, :], VR[:, s, k * 512:(k + 1) * 512],
                                            start=(s == 0), stop=(s == GROUP - 1))
                        ins.then_inc(S("v_used"), 1)

            pe.sem_inc(S("v_used"), 1)
            with pe.Fori(0, TB * PH) as i:
                peer_pe(i)
            pe.wait_ge(S("peer_added"), 32 * TB + 1)
            stage_end(pe, 3)
            pe_transposes(pe, "mT", lambda b, c: XN2[:, b, c * P:(c + 1) * P],
                          lambda: pe.wait_ge(S("pre_scaled"), TB))
            for c in range(KC):
                read_out(pe, ("mT", c))

            def xt(k):
                return pair(XT[:, k, :], XL4[:, k, :])

            def xtb(k, b):
                return pair(XT[:, k, b * P:(b + 1) * P], XL4[:, k, b * P:(b + 1) * P])

            for n in range(2):
                w = split_in(pe, f"w2_q{n}")
                pe_feature(pe, "q2", 2 * n, w, 256, (0, P), xt, T)
                tile_done(f"w2_q{n}", ("q2", 2 * n + 1))
            w = split_in(pe, "w2_kv0")
            pe_feature(pe, "kv2", 0, w, 256, (0, P), xt, T)
            tile_done("w2_kv0", ("kv2", 1))
            w = split_in(pe, "w2_kv1")
            pe_feature(pe, "kv2", 2, w, 256, (0,), xt, T)
            pe_token(pe, "vs", w, 256, 128, 128, xtb)
            tile_done("w2_kv1", ("vs", TB - 1))
            w = split_in(pe, "w2_kw")
            pe_feature(pe, "kw", 0, w, 128, (0,), xt, T)
            tile_done("w2_kw", ("kw", 0))
            w = split_in(pe, "w2_vwg")
            pe_token(pe, "vwg", w, 152, 0, 152, xtb)
            tile_done("w2_vwg", ("vwg", TB - 1))
            pe_token_rows(pe, [("cq", b) for b in range(TB)], ["w2_cq_0", "w2_cq_1"], (4, 4), 384, xtb)
            w = split_in(pe, "w2_kr")
            ps = take(pe, "kr")
            for k in range(KC):
                ins = mm3(pe, ps[0:96, :], cut(w, k * 96, (k + 1) * 96), xt(k), k == 0, k == KC - 1)
            fin(ins, "kr")
            tile_done("w2_kr", "kr")
            for j, name in enumerate(("ck", "cv")):
                w = tile_in(pe, name + "_w1")
                pe.wait_ge(S("blocks_ready"), j + 1)
                ps = take(pe, name + "1")
                for l in range(CMP_L):
                    ins = pe.matmul(ps[:, 0:NCMP], w[:, l * P:(l + 1) * P], PB[:, j, l, :],
                                    start=(l == 0), stop=(l == CMP_L - 1))
                fin(ins, name + "1")
                tile_done(name + "_w1", name + "1")
            pe.wait_ge(S("hid_zero"), 1)
            read_out(pe, "ck1")
            ps = take(pe, "ck2")
            fin(pe.matmul(ps[:, 0:NCMP], V("ck_w2"), HID[:, 0, 0:NCMP], start=True, stop=True), "ck2")
            read_out(pe, "cv1")
            ps = take(pe, "cv2")
            for r in range(4):
                ins = pe.matmul(ps[32 * r:32 * r + 32, 0:P], HID[:, 1, :], V("cv_w2"), start=True, stop=True)
            fin(ins, "cv2")
            pe_feature_tiles(pe, "mg", [f"w2_merge{n}" for n in range(8)], xt)
            for m in range(4):
                read_out(pe, ("q2", m))
            read_out(pe, "ck2")

            def cmp_scores(b):
                for g in range(G):
                    rows = slice(64 * g, 64 * g + 64)
                    ps = take(pe, ("cs", b, g))
                    for r in range(4):
                        ins = pe.matmul(ps[:, r * NCMP:(r + 1) * NCMP], QN[rows, r, b * P:(b + 1) * P],
                                        KCMP[rows, 0:NCMP], start=True, stop=True)
                    fin(ins, ("cs", b, g))

            cmp_scores(0)
            for b in range(TB):
                if b + 1 < TB:
                    cmp_scores(b + 1)
                pe.wait_ge(S("pc_ready"), b + 1)
                ps = take(pe, ("pcT", b))
                for g in range(G):
                    ins = pe.transpose(ps[:, g * P:(g + 1) * P],
                                       PC[:, b % 2, 4 * g:4 * g + 4, :].rearrange("p h j -> p (h j)"), ident)
                fin(ins, ("pcT", b))
            for n in range(3):
                read_out(pe, ("kv2", n))
            read_out(pe, ("kw", 0))
            for b in range(TB):
                read_out(pe, ("vs", b))
                read_out(pe, ("vwg", b))
                read_out(pe, ("pcT", b))
            read_out(pe, "cv2")

            def causal_scores(name, u, b, q, k):
                ps = take(pe, (name, u))
                fin(pe.matmul(ps[:, 0:(b + 1) * P], q, k, start=True, stop=True), (name, u))

            def causal_transposes(name, u, b):
                pe.wait_ge(S(name + "_p"), u + 1)
                ps = take(pe, (name + "T", u))
                for s in range(b + 1):
                    ins = pe.transpose(ps[:, s * P:(s + 1) * P], unit_rows(u)[:, s * P:(s + 1) * P], ident)
                fin(ins, (name + "T", u))

            def causal_values(pe, ps, rows, buf, v, first, last):
                for s in range(TB):
                    ins = pe.matmul(ps[rows, s * P:T], v(s), PT[:, buf, s, s * P:T],
                                    start=(first and s == 0), stop=(last and s == TB - 1))
                return ins

            def n_scores(u):
                hb, b = divmod(u, TB)
                n, br = divmod(hb, 2)
                m, g = divmod(n, 2)
                rows = slice(64 * g, 64 * g + 64)
                causal_scores("n", u, b, QN[rows, m, b * P:(b + 1) * P], KX[rows, 2 + br, 0:(b + 1) * P])

            def n_values(n):
                m, g = divmod(n, 2)
                for u in range(8 * n, 8 * n + 8):
                    read_out(pe, ("nT", u))
                rows, cols = slice(64 * g, 64 * g + 64), slice(64 * g, 64 * g + 64)
                ps = take(pe, ("no", n))
                pe.matmul(ps[rows, :], VC4[32 * m:32 * m + 32, cols], PCT[32 * m:32 * m + 32, g, :],
                          start=True, stop=False)
                for br in range(2):
                    ins = causal_values(pe, ps, rows, (2 * n + br) % 3, lambda s: VX[:, br, s, cols], False, br == 1)
                fin(ins, ("no", n))

            for u in range(SCORES_AHEAD):
                n_scores(u)
            for u in range(64):
                if u + SCORES_AHEAD < 64:
                    n_scores(u + SCORES_AHEAD)
                causal_transposes("n", u, u % TB)
                if u % 8 == 3 and u > 8:
                    n_values(u // 8 - 1)
            n_values(7)
            stage_end(pe, 4)
            pe.wait_ge(S("cq_scaled"), 2 * TB)
            for c in range(3):
                ps = take(pe, ("cqT", c))
                for b in range(TB):
                    ins = pe.transpose(ps[:, b * P:(b + 1) * P], CQ[:, b, c * P:(c + 1) * P], ident)
                fin(ins, ("cqT", c))
            for c in range(3):
                read_out(pe, ("cqT", c))
            w = tile_in(pe, "w_uq")
            for h in range(NH):
                ps = take(pe, ("uq", h))
                for k in range(2):
                    ins = pe.matmul(ps[0:96, :], w[:, k * 768 + h * 96:k * 768 + h * 96 + 96], XT[:, k, :],
                                    start=(k == 0), stop=(k == 1))
                fin(ins, ("uq", h))
            tile_done("w_uq", ("uq", NH - 1))
            w = tile_in(pe, "w_ukv")
            for h in range(NH):
                ps = take(pe, ("uk", h))
                fin(pe.matmul(ps[0:64, :], w[:, h * P:h * P + 64], XT[:, 2, :], start=True, stop=True), ("uk", h))
            wv = w[:, 0:1024].rearrange("p (h d) -> p h d", h=NH)[:, :, 64:128]
            for b in range(TB):
                ps = take(pe, ("uv", b))
                fin(pe.matmul(ps[:], XT[:, 2, b * P:(b + 1) * P], wv, start=True, stop=True), ("uv", b))
            tile_done("w_ukv", ("uv", TB - 1))
            def rope_product(h):
                src = KR if h == 0 else QM[:, h - 1, :]
                if h:
                    read_out(pe, ("uq", h - 1))
                ps = take(pe, ("rope", h))
                fin(pe.matmul(ps[64:96, :], V("rot")[64:96, :], src[64:96, :], start=True, stop=True), ("rope", h))
            for h in range(4):
                rope_product(h)
            pe.wait_ge(S("k_roped"), NH)
            for h in range(NH):
                read_out(pe, ("uk", h))
            for b in range(TB):
                read_out(pe, ("uv", b))

            def m_scores(u):
                h, b = divmod(u, TB)
                pe.wait_ge(S("q_roped"), h + 1)
                causal_scores("m", u, b, QM[0:96, h, b * P:(b + 1) * P], KM[0:96, h, 0:(b + 1) * P])

            def m_values(h):
                for u in range(TB * h, TB * h + TB):
                    read_out(pe, ("mT2", u))
                rows = slice(64 * (h % 2), 64 * (h % 2) + 64)
                ps = take(pe, ("mo2", h))
                fin(causal_values(pe, ps, rows, h % 3, lambda s: VM[:, s, 64 * h:64 * h + 64], True, True), ("mo2", h))

            def m_transposes(u):
                pe.wait_ge(S("m_p"), u + 1)
                b = u % TB
                ps = take(pe, ("mT2", u))
                for s in range(b + 1):
                    ins = pe.transpose(ps[:, s * P:(s + 1) * P], unit_rows(u)[:, s * P:(s + 1) * P], ident)
                fin(ins, ("mT2", u))

            for u in range(SCORES_AHEAD):
                m_scores(u)
            for u in range(32):
                if u + SCORES_AHEAD < 32:
                    m_scores(u + SCORES_AHEAD)
                if u % 4 == 2 and u // 4 + 4 <= NH:
                    rope_product(u // 4 + 4)
                m_transposes(u)
                if u % 4 == 2 and u > 4:
                    m_values(u // 4 - 1)
            m_values(7)
            for n in range(NH):
                read_out(pe, ("no", n))
                read_out(pe, ("mo2", n))
            wn = tile_in(pe, "w_br_nsa")
            wm = tile_in(pe, "w_br_mla")
            for c in range(KC):
                for name, w, src in (("bn", wn, ON), ("bm", wm, OM)):
                    ps = take(pe, (name, c))
                    for k in range(4):
                        ins = pe.matmul(ps[:], w[:, k * D + c * P:k * D + (c + 1) * P], src[:, k, :],
                                        start=(k == 0), stop=(k == 3))
                    fin(ins, (name, c))
            tile_done("w_br_nsa", ("bn", KC - 1))
            tile_done("w_br_mla", ("bm", KC - 1))
            pe.wait_ge(S("merged_low"), KC)
            for n in range(2):
                pe_token_rows(pe, [(("wo", n), b) for b in range(TB)], [f"w_o{n}_0", f"w_o{n}_1"], (4, 4), 512,
                              lambda k, b: pair(MGH[:, k, b * P:(b + 1) * P], MG[:, k, b * P:(b + 1) * P]))
            stage_end(pe, 5)
            pe_transposes(pe, "fT", lambda b, c: FX[:, b, c * P:(c + 1) * P],
                          lambda: pe.wait_ge(S("ffn_scaled"), TB))
            for c in range(KC):
                read_out(pe, ("fT", c))
            pe_feature_tiles(pe, "up", [f"w_up{n}" for n in range(22)],
                             lambda k: pair(XT[:, k, :], XL5[:, k, :]))
            pe.wait_ge(S("mf_low"), FC)
            for n in range(2):
                pe_token_rows(pe, [("dn", n, b) for b in range(TB)], [f"w_down{n}_{k}" for k in range(6)], DOWN_ROWS,
                              512, lambda k, b: pair(MFH(k)[:, b * P:(b + 1) * P], MF[:, k, b * P:(b + 1) * P]))
            stage_end(pe, 6)
            pe.wait_ge(S("ple_landed"), 16)
            for c in range(2):
                ps = take(pe, ("plT", c))
                for b in range(TB):
                    ins = pe.transpose(ps[:, b * P:(b + 1) * P], PI[:, b, c * P:(c + 1) * P], ident)
                fin(ins, ("plT", c))
            pe_transposes(pe, "hT", lambda b, c: H[:, b, c * P:(c + 1) * P], lambda: pe.wait_ge(S("ffn_added"), TB))
            for c in range(2):
                read_out(pe, ("plT", c))
            for c in range(KC):
                read_out(pe, ("hT", c))
            for n in range(2):
                pe_token_rows(pe, [("pg", n, b) for b in range(TB)], [f"w_pg{n}_0", f"w_pg{n}_1"], (4, 4), 512,
                              lambda k, b: pair(XT[:, k, b * P:(b + 1) * P], XL5[:, k, b * P:(b + 1) * P]))
                wp = tile_in(pe, f"w_ple{n}")
                for b in range(TB):
                    ps = take(pe, ("pe", n, b))
                    for k in range(2):
                        ins = pe.matmul(ps[:], PLT[:, k, b * P:(b + 1) * P],
                                        wp[:, k * 512:(k + 1) * 512], start=(k == 0), stop=(k == 1))
                    fin(ins, ("pe", n, b))
                tile_done(f"w_ple{n}", ("pe", n, TB - 1))

        @block.scalar
        def _(act):
            act.wait_ge(S("x_landed"), 16)
            act_norm(act, "mix", lambda b: H[:, b, :], lambda b: XN1[:, b, :], 0)
            act.wait_ge(S("vec_landed"), 16)
            for c in range(KC):
                act_high(act, "mixT", ("mixT", c), XT[:, c, :], c, scale=V("norm_mix", c, c + 1))
            ps = full(act, "beta")
            read(act.activation(ROWS[0:4, 2, :], ps[0:4, :], ACT.Sigmoid), "beta")
            act.wait_ge(S("a_abs"), 1)
            act.activation(ROWT[0:4, 2, :], ROWT[0:4, 1, :], ACT.Exp, scale=-1.0).then_inc(S("row_act"), 1)
            act.wait_ge(S("row_act"), 1)
            act.activation(ROWT[0:4, 3, :], ROWT[0:4, 2, :], ACT.Ln, bias=ones[0:4, 0:1]).then_inc(S("row_act"), 1)
            act.activation(stats[0:4, 90:91], V("a_log")[0:4, :], ACT.Exp).then_inc(S("row_act"), 1)
            for n, dst in ((0, BT), (1, CT)):
                for m in range(4):
                    ps = full(act, (("proj", n), m))
                    read(act.activation(dst[:, m, :], ps[:], ACT.Copy), (("proj", n), m))
            act.wait_ge(S("g_cumsum"), 1)
            act.activation(ROWS[0:4, 1, :], ROWS[0:4, 0, :], ACT.Exp).then_inc(S("row_exp"), 1)
            act.wait_ge(S("g_rest"), 1)
            act.activation(ROWS[0:4, 4, :], ROWT[0:4, 0, :], ACT.Exp).then_inc(S("row_exp"), 1)
            for j in range(12):
                act.wait_ge(S("qkv_conv"), j + 1)
                act.activation(QKV[:, j, :], CONVT[:, j % 2, :], ACT.Silu)\
                   .then_inc(S("qkv_silu" if j < 8 else "v_done"), 1)
            for m in range(4):
                ps = full(act, (("proj", 6), m))
                read(act.activation(ZT[:, m, :], ps[:], ACT.Silu), (("proj", 6), m))
            for j in range(8):
                act.wait_ge(S("qkv_silu"), j + 1)
                if j >= 2:
                    full(act, ("l2", j - 2))
                act.activation(LSQ[:, j % 2, :], QKV[:, j, :], ACT.Square).then_inc(S("qk_squared"), 1)
                ps = full(act, ("l2", j))
                if j >= 2:
                    act.wait_ge(S("l2_inv"), j - 1)
                read(act.activation(LRT[:, j % 2, :], ps[:], ACT.Sqrt, bias=eps), ("l2", j))
            for r, dst in ((0, GB), (1, EGB), (2, BB)):
                for h in range(DN_H):
                    ps = full(act, ("rowb", r, h))
                    read(act.activation(dst[:, h, :], ps[:], ACT.Copy), ("rowb", r, h))
            ps = full(act, "tok")
            read(act.activation(TOK, ps[:, 0:64], ACT.Copy), "tok")
            for b in range(TB):
                act.wait_ge(S("decay_arg"), 4 * (b + 1))
                act.activation(DT[:, b, :, :], DT[:, b, :, :], ACT.Exp).then_inc(S("decay_exp"), 1)
            for b in range(TB):
                ps = full(act, ("t0", b))
                read(act.activation(TM[:, b, :, :], ps[:], ACT.Copy), ("t0", b))
            for lv in range(1, 6):
                for b in range(TB):
                    ps = full(act, ("x", lv, b))
                    if lv > 1:
                        full(act, ("dtt", lv - 1, b))
                    else:
                        act.wait_ge(S("a_done"), TB)
                    read(act.activation(XM[:, b, :], ps[:], ACT.Copy), ("x", lv, b))
            for b in range(TB):
                ps = full(act, ("u", b))
                read(act.activation(UU[:, b, :, :], ps[:], ACT.Copy), ("u", b))
                ps = full(act, ("w", b))
                act.wait_ge(S("c_masked"), 5 * TB)
                read(act.activation(WT[:, b, :, :], ps[:], ACT.Copy), ("w", b))
            for k in range(4):
                act.wait_ge(S("yconv_done"), k + 1)
                act.activation(rounded(YH(k)), YT[:, k, :], ACT.Copy).then_inc(S("y_high"), 1)
            act.wait_ge(S("mem_landed"), 16)
            for b in range(2):
                act.activation(MEMN[:, b, :], MEMX[:, b, :], ACT.Square, accum_out=stat(3, 2)[:, b:b + 1])\
                   .then_inc(S("norm_sumsq"), 1)
            for c in range(8):
                if c == 4:
                    act.wait_ge(S("norm_meansq"), norm_no["mem"] + 1)
                    act.activation(stat(4, 2), stat(3, 2), ACT.Sqrt).then_inc(S("norm_root"), 1)
                ps = full(act, ("o", c))
                read(act.activation(OT[:, :, c * CHUNK:(c + 1) * CHUNK],
                                    ps[:, 0:256].rearrange("p (h i) -> p h i", h=DN_H), ACT.Copy), ("o", c))
            for c in range(8):
                read_out(act, ("o", c))
            full(act, ("kv", 7))
            for h in range(DN_H):
                if h >= 2:
                    full(act, ("on", h - 2))
                act.activation(LSQ[:, h % 2, :], OT[:, h, :], ACT.Square).then_inc(S("o_squared"), 1)
                ps = full(act, ("on", h))
                if h >= 2:
                    act.wait_ge(S("on_inv"), h - 1)
                read(act.activation(LRT[:, h % 2, :], ps[:], ACT.Sqrt, scale=1.0 / P, bias=eps), ("on", h))
            for c in range(KC):
                act_high(act, "memT", ("memT", c), MT[:, c, :], c, scale=V("norm_mem", c, c + 1))
            for h in range(DN_H):
                act.wait_ge(S("ydn_done"), h + 1)
                act.activation(rounded(YH(4 + h)), YT[:, 4 + h, :], ACT.Copy).then_inc(S("y_high"), 1)
            stage_end(act, 1)
            act_norm(act, "x", lambda b: H[:, b, :], lambda b: XNX[:, b, :], 6)
            for n in range(2):
                for m in range(4):
                    ps = full(act, (("xk", n), m))
                    read(act.activation(MK[:, 4 * n + m, :], ps[:, 0:MEM], ACT.Copy), (("xk", n), m))
                    if m % 2:
                        act_tile_high(act, ACT_HIGHS[2 * n + m // 2])
            act_tile_high(act, "w_xv1_1")
            for n in range(2):
                for b in range(2):
                    ps = full(act, (("xv", n), b))
                    read(act.activation(MV[:, b, n * 512:(n + 1) * 512], ps[:], ACT.Copy), (("xv", n), b))
            for c in range(KC):
                act_high(act, "xT", ("xT", c), XT[:, c, :], c, scale=V("norm_x", c, c + 1))
            for n in range(2):
                for m in range(4):
                    ps = full(act, (("xq", n), m))
                    read(act.activation(XQ[:, 4 * n + m, :], ps[:], ACT.Copy, scale=256.0 ** -0.5), (("xq", n), m))

            def x_transposed(u):
                hp, b = divmod(u, TB)
                ps = full(act, ("xpT", u))
                read(act.activation(XPT[:, 4 * hp:4 * hp + 4, b * P:(b + 1) * P],
                                    ps[:].rearrange("p (j i) -> p j i", j=4), ACT.Copy), ("xpT", u))

            for u in range(8):
                ps = full(act, ("xs", u))
                act.wait_ge(S("x_max"), u + 1)
                if u >= 4:
                    full(act, ("xpT", u - 4))
                st = 160 + 8 * (u % 4)
                for h2 in range(2):
                    ins = act.activation(XP[u % 4][:, h2, :], ps[:, h2 * MEM:(h2 + 1) * MEM], ACT.Exp,
                                         bias=stats[:, st + h2:st + h2 + 1],
                                         accum_out=stats[:, st + 2 + h2:st + 3 + h2])
                    if h2:
                        read(ins, ("xs", u))
                    else:
                        ins.then_inc(S("x_exp"), 1)
                if u >= 2:
                    x_transposed(u - 2)
            x_transposed(6)
            x_transposed(7)
            for h in range(X_H):
                for dc in range(2):
                    act_high(act, "xo", ("xo", h, dc), XO[:, 2 * h + dc, :], 2 * h + dc)
            act_norm(act, "peer", lambda b: H[:, b, :], lambda b: PX[:, b, :], 9,
                     ready=lambda e, b: read_out(e, (("xout", 1), b)))
            stage_end(act, 2)
            for c in range(KC):
                act_high(act, "pT", ("pT", c), XT[:, c, :], c)
            for n in range(2):
                for m in range(4):
                    ps = full(act, (("pq", n), m))
                    read(act.activation(PQ[:, 4 * n + m, :], ps[:], ACT.Copy), (("pq", n), m))
            for b in range(TB):
                for hp in range(4):
                    ps = full(act, ("ps", b, hp))
                    at = b * PH * NKEY + hp // 2 * 512
                    read(act.activation(SC[:, hp % 2, at:at + 512], ps[:], ACT.Copy), ("ps", b, hp))

            def topk_act(n):
                act.wait_ge(S("topk_best"), n + 1)
                act.activation(GE, BEST, ACT.Exp, bias=NB, accum_out=GSUM).then_inc(S("topk_exp"), 1)

            def peer_act(i, ahead=True):
                for par in range(2):
                    g = 2 * i + par
                    act.wait_ge(S("dots_done"), GROUP * g + (GROUP + 1))
                    act.activation(ACTS[:, par, :], DOTS[:, par, :], ACT.Gelu).then_inc(S("gelu_done"), 1)
                    act.wait_ge(S("gated"), g + 1)
                    act.wait_ge(S("v_used"), GROUP * g + 1)
                    for s in range(GROUP):
                        act.activation(DIAG[:, s, :], ident, ACT.Copy, scale=W8[:, par, s:s + 1])\
                           .then_inc(S("diag_made"), 1)
                if ahead:
                    topk_act(i + AHEAD)

            for n in range(AHEAD):
                topk_act(n)
            with act.Fori(0, TB * PH - AHEAD) as i:
                peer_act(i)
            with act.Fori(TB * PH - AHEAD, TB * PH) as i:
                peer_act(i, ahead=False)
            act_norm(act, "final", lambda b: H[:, b, :], lambda b: FSQ[:, b, :], 12,
                     ready=lambda e, b: e.wait_ge(S("peer_added"), 32 * (b + 1) + 1))
            stage_end(act, 3)
            act_norm(act, "pre", lambda b: H[:, b, :], lambda b: XN2[:, b, :], 15,
                     ready=lambda e, b: e.wait_ge(S("final_scaled"), b + 1))
            for c in range(KC):
                act_high(act, "mT", ("mT", c), XT[:, c, :], c, scale=V("pre_mix", c, c + 1))
            for m in range(4):
                ps = full(act, ("q2", m))
                read(act.activation(QN[:, m, :], ps[:], ACT.Copy, scale=V("q_scale", m, m + 1)), ("q2", m))
                if m % 2:
                    act_tile_high(act, ("w2_kv1", "w2_kw")[m // 2])
            act.wait_ge(S("angles"), 2)
            act.activation(SIN[64:96, :], SIN[64:96, :], ACT.Sin).then_inc(S("rope_table"), 1)
            act.activation(COS[64:96, :], COS[64:96, :], ACT.Sin).then_inc(S("rope_table"), 1)
            for n in range(3):
                ps = full(act, ("kv2", n))
                read(act.activation(KX[:, n, :], ps[:], ACT.Copy), ("kv2", n))
                if n == 1:
                    act_tile_high(act, "w2_vwg")
            for b in range(TB):
                ps = full(act, ("vs", b))
                read(act.activation(VX[:, 0, b, :], ps[:, 0:P], ACT.Copy), ("vs", b))
            act_tile_high(act, "w2_cq_0")
            ps = full(act, ("kw", 0))
            read(act.activation(KX[:, 3, :], ps[:], ACT.Copy), ("kw", 0))
            act_tile_high(act, "w2_cq_1")
            for b in range(TB):
                ps = full(act, ("vwg", b))
                act.activation(VX[:, 1, b, :], ps[:, 0:P], ACT.Copy).then_inc(S("vw_copied"), 1)
                read(act.activation(GT[:, b, :], ps[:, P:P + 24], ACT.Sigmoid), ("vwg", b))
            act_tile_high(act, "w2_kr")
            for b in range(TB):
                ps = full(act, ("cq", b))
                read(act.activation(CQ[:, b, :], ps[:, 0:384], ACT.Copy), ("cq", b))
            ps = full(act, "kr")
            read(act.activation(KR[64:96, :], ps[64:96, :], ACT.Copy), "kr")
            for j, name in enumerate(("ck", "cv")):
                ps = full(act, name + "1")
                read(act.activation(HID[:, j, 0:NCMP], ps[:, 0:NCMP], ACT.Gelu_apprx_tanh, bias=V(name + "_b1")),
                     name + "1")
            ps = full(act, "ck2")
            read(act.activation(KCMP[:, 0:NCMP], ps[:, 0:NCMP], ACT.Copy), "ck2")
            ps = full(act, "cv2")
            read(act.activation(VC4, ps[:, 0:P], ACT.Copy), "cv2")
            for n in range(4):
                for m in range(4):
                    ps = full(act, (("mg", n), m))
                    read(act.activation(GM[:, 4 * n + m, :], ps[:], ACT.Sigmoid), (("mg", n), m))
            for b in range(TB):
                act.wait_ge(S("cmp_min"), NH * (b + 1))
                st = 256 + 32 * (b % 2)
                for h in range(NH):
                    act.activation(PC[:, b % 2, h, 0:NCMP], PC[:, b % 2, h, 0:NCMP], ACT.Exp, scale=-1.0,
                                   bias=stats[:, st + h:st + h + 1], accum_out=stats[:, st + 8 + h:st + 9 + h])\
                       .then_inc(S("cmp_exp"), 1)
            for b in range(TB):
                ps = full(act, ("pcT", b))
                read(act.activation(PCT[:, :, b * P:(b + 1) * P], ps[:, 0:256].rearrange("p (g i) -> p g i", g=G),
                                    ACT.Copy), ("pcT", b))

            def soft_exp(name, u, b):
                act.wait_ge(S(name + "_min"), u + 1)
                st = 224 + 4 * (u % 4)
                p = unit_rows(u)[:, 0:(b + 1) * P]
                act.activation(p, p, ACT.Exp, scale=-1.0, bias=stats[:, st:st + 1],
                               accum_out=stats[:, st + 1:st + 2]).then_inc(S(name + "_exp"), 1)

            def soft_transposed(prod, u, b, buf):
                ps = full(act, (prod, u))
                read(act.activation(PT[:, buf, 0:b + 1, b * P:(b + 1) * P],
                                    ps[:, 0:(b + 1) * P].rearrange("p (s i) -> p s i", i=P), ACT.Copy), (prod, u))

            def n_transposed(u):
                n = u // 8
                if u % 8 == 4 and n:
                    full(act, ("no", n - 1))
                soft_transposed("nT", u, u % TB, (u // 4) % 3)

            def n_out(n):
                m, g = divmod(n, 2)
                ps = full(act, ("no", n))
                read(act.activation(ON[64 * g:64 * g + 64, m, :], ps[64 * g:64 * g + 64, :], ACT.Copy), ("no", n))

            for u in range(64):
                soft_exp("n", u, u % TB)
                if u >= 2:
                    n_transposed(u - 2)
                if u % 8 == 5 and u > 8:
                    n_out(u // 8 - 1)
            n_transposed(62)
            n_transposed(63)
            n_out(7)
            stage_end(act, 4)
            for j, (a, b_, name) in enumerate(((0, 256, "cq"), (256, 384, "ckv"))):
                for b in range(TB):
                    act.activation(SQ2[:, b, a:b_], CQ[:, b, a:b_], ACT.Square,
                                   accum_out=stat(18 + 3 * j)[:, b:b + 1]).then_inc(S("norm_sumsq"), 1)
            for j, name in enumerate(("cq", "ckv")):
                act.wait_ge(S("norm_meansq"), norm_no[name] + 1)
                act.activation(stat(19 + 3 * j), stat(18 + 3 * j), ACT.Sqrt).then_inc(S("norm_root"), 1)
            for c in range(3):
                ps = full(act, ("cqT", c))
                gain = V("g_q", c, c + 1) if c < 2 else V("g_kv")
                read(act.activation(XT[:, c, :], ps[:], ACT.Copy, scale=gain), ("cqT", c))
            for h in range(NH):
                ps = full(act, ("uq", h))
                read(act.activation(QM[0:96, h, :], ps[0:96, :], ACT.Copy), ("uq", h))
            for h in range(NH):
                ps = full(act, ("uk", h))
                read(act.activation(KM[0:64, h, :], ps[0:64, :], ACT.Copy), ("uk", h))
            for b in range(TB):
                ps = full(act, ("uv", b))
                read(act.activation(VM[:, b, :], ps[:], ACT.Copy), ("uv", b))

            def m_transposed(u):
                h = u // TB
                if u % TB == 0 and h > 2:
                    full(act, ("mo2", h - 3))
                soft_transposed("mT2", u, u % TB, h % 3)

            def m_out(h):
                rows = slice(64 * (h % 2), 64 * (h % 2) + 64)
                ps = full(act, ("mo2", h))
                read(act.activation(OM[rows, h // 2, :], ps[rows, :], ACT.Copy), ("mo2", h))

            for u in range(32):
                soft_exp("m", u, u % TB)
                if u >= 2:
                    m_transposed(u - 2)
                if u % TB == 3 and u > TB:
                    m_out(u // TB - 1)
            m_transposed(30)
            m_transposed(31)
            m_out(7)
            for c in range(KC):
                act.wait_ge(S("merged"), c + 1)
                act.activation(rounded(MGH[:, c, :]), MG[:, c, :], ACT.Copy).then_inc(S("merged_high"), 1)
            for n in range(2):
                for b in range(TB):
                    ps = full(act, (("wo", n), b))
                    read(act.activation(YB[:, b, n * 512:(n + 1) * 512], ps[:], ACT.Copy), (("wo", n), b))
            for n in range(2):
                for b in range(TB):
                    read_out(act, (("wo", n), b))
            act_norm(act, "post", lambda b: YB[:, b, :], lambda b: XN2[:, b, :], 24)
            act_norm(act, "ffn", lambda b: H[:, b, :], lambda b: FFN_SQ[:, b, :], 12,
                     ready=lambda e, b: e.wait_ge(S("mix2_added"), b + 1))
            stage_end(act, 5)
            for c in range(KC):
                act_high(act, "fT", ("fT", c), XT[:, c, :], c, scale=V("pre_ffn", c, c + 1))

            def up_gelu(n):
                for m in range(2):
                    act.wait_ge(S("up_conv"), 4 * n + m + 1)
                    act.activation(AC[:, n % 2, m, :], AC[:, n % 2, m, :], ACT.Gelu_apprx_tanh)\
                       .then_inc(S("up_gelu"), 1)

            def up_high(n):
                for k in range(2 * n, 2 * n + 2):
                    act.wait_ge(S("mf_ready"), k + 1)
                    act.activation(rounded(MFH(k)), MF[:, k, :], ACT.Copy).then_inc(S("mf_high"), 1)

            for n in range(11):
                for m in range(4):
                    c = 2 * n + m % 2 + FC * (m // 2)
                    ps = full(act, (("up", n), m))
                    if n >= 2:
                        act.wait_ge(S("mf_ready"), 2 * (n - 1))
                    act.activation(AC[:, n % 2, m, :], ps[:], ACT.Identity, scale=V("up_conv", 3 * c + 2, 3 * c + 3),
                                   bias=V("up_b", c, c + 1)).then_inc(S("up_affine"), 1)
                    if m % 2:
                        act_tile_high(act, FFN_TILES[2 * n + m // 2 + SLOTS])
                if n:
                    up_gelu(n - 1)
                if n >= 2:
                    up_high(n - 2)
            up_gelu(10)
            up_high(9)
            up_high(10)
            for n in range(2):
                for name in FFN_TILES[25:31] if n == 0 else FFN_TILES[31:]:
                    act_tile_high(act, name)
                for b in range(TB):
                    ps = full(act, ("dn", n, b))
                    read(act.activation(YF[:, b, n * 512:(n + 1) * 512], ps[:], ACT.Copy), ("dn", n, b))
            for n in range(2):
                for b in range(TB):
                    read_out(act, ("dn", n, b))
            act_norm(act, "down", lambda b: YF[:, b, :], lambda b: FX[:, b, :], 15)
            stage_end(act, 6)
            for c in range(2):
                ps = full(act, ("plT", c))
                read(act.activation(PLT[:, c, :], ps[:], ACT.Copy), ("plT", c))
            for c in range(KC):
                act_high(act, "hT", ("hT", c), XT[:, c, :], c)
            for n in range(2):
                for b in range(TB):
                    j = TB * n + b
                    ps = full(act, ("pg", n, b))
                    if j >= 2:
                        act.wait_ge(S("ple_gated"), j - 1)
                    read(act.activation(SG[:, j % 2, :], ps[:], ACT.Sigmoid), ("pg", n, b))
            act_norm(act, "ple", lambda b: YP[:, b, :], lambda b: FQ[:, b, :], 18,
                     ready=lambda e, b: e.wait_ge(S("ple_gated"), TB + b + 1))

        @block.vector
        def _(dve):
            links = [0]

            def link(ins):
                links[0] += 1
                ins.then_inc(S("dve_link"), 1)
                dve.wait_ge(S("dve_link"), links[0])

            dve.wait_ge(S("x_landed"), 16)
            rs = dve_norm_scale(dve, "mix", 0, D)
            for b in range(TB):
                dve.tensor_scalar(XN1[:, b, :], H[:, b, :], rs[:, b:b + 1], None, ALU.mult)\
                   .then_inc(S("mix_scaled"), 1)
            dve.wait_ge(S("vec_landed"), 16)
            dve.tensor_copy(WBA[0][:], V("w_ba")).then_inc(S("ba_split"), 1)
            dve.wait_ge(S("ba_split"), 1)
            dve.tensor_tensor(WBA[1][:], V("w_ba"), WBA[0][:].bitcast(F32), ALU.subtract).then_inc(S("ba_split"), 1)
            for c in range(KC):
                dve_low(dve, "mixT", ("mixT", c), XT[:, c, :], XL1[:, c, :], c, scale=V("norm_mix", c, c + 1))
            ps = full(dve, "a")
            read(dve.tensor_scalar(ROWT[0:4, 0, :], ps[0:4, :], V("dt_bias")[0:4, :], None, ALU.add), "a")
            read_out(dve, "a")
            dve.scalar_tensor_tensor(out=ROWT[0:4, 1, :], in0=ROWT[0:4, 0, :], scalar=-1.0, in1=ROWT[0:4, 0, :],
                                     op0=ALU.mult, op1=ALU.max).then_inc(S("a_abs"), 1)
            dve.wait_ge(S("row_act"), 3)
            link(dve.scalar_tensor_tensor(out=ROWT[0:4, 0, :], in0=ROWT[0:4, 0, :], scalar=0.0, in1=ROWT[0:4, 3, :],
                                          op0=ALU.max, op1=ALU.add))
            link(dve.tensor_scalar(ROWT[0:4, 0, :], ROWT[0:4, 0, :], stats[0:4, 90:91], -1.0, ALU.mult, ALU.mult))
            dve.wait_ge(S("gdn_landed"), 16)
            dve.tensor_tensor_scan(ROWS[0:4, 0, :], gd("restart")[0:4, :], ROWT[0:4, 0, :], 0.0, ALU.mult, ALU.add)\
               .then_inc(S("g_cumsum"), 1)
            dve.wait_ge(S("g_cumsum"), 1)
            g4 = ROWS[0:4, 0, :].rearrange("p (c i) -> p c i", i=CHUNK)
            dve.tensor_tensor(ROWT[0:4, 0, :].rearrange("p (c i) -> p c i", i=CHUNK),
                              g4[:, :, CHUNK - 1:CHUNK].to_broadcast([4, 8, CHUNK]), g4, ALU.subtract)\
               .then_inc(S("g_rest"), 1)
            read_out(dve, "beta")
            dve.wait_ge(S("row_exp"), 2)
            dve.tensor_tensor(ROWS[0:4, 3, :], ROWS[0:4, 1, :], ROWS[0:4, 2, :], ALU.mult).then_inc(S("rows_done"), 1)
            for m in range(4):
                ps = full(dve, (("proj", 2), m))
                read_out(dve, (("proj", 1), m))
                read(dve.tensor_tensor(CT[:, m, :], ps[:], CT[:, m, :], ALU.mult), (("proj", 2), m))
                read_out(dve, (("proj", 2), m))
                w = [V("conv_w", 3 * m + j, 3 * m + j + 1) for j in range(3)]
                link(dve.tensor_scalar(YT[:, m, :], CT[:, m, :], w[2], None, ALU.mult))
                for s in (1, 2):
                    link(dve.scalar_tensor_tensor(out=YT[:, m, s:T], in0=CT[:, m, 0:T - s], scalar=w[2 - s],
                                                  in1=YT[:, m, s:T], op0=ALU.mult, op1=ALU.add))
                read_out(dve, (("proj", 0), m))
                dve.tensor_tensor(YT[:, m, :], YT[:, m, :], BT[:, m, :], ALU.mult).then_inc(S("yconv_done"), 1)
            for j in range(12):
                name = (("proj", 3 + j // 4), j % 4)
                ps = full(dve, name)
                w = [V("dn_conv_w", 4 * j + t, 4 * j + t + 1) for t in range(4)]
                if j >= 2:
                    if j - 2 < 8:
                        dve.wait_ge(S("qkv_silu"), j - 1)
                    else:
                        dve.wait_ge(S("v_done"), j - 9)
                acc = CONVT[:, j % 2, :]
                link(dve.tensor_scalar(acc, ps[:], w[3], None, ALU.mult))
                for s in (1, 2):
                    link(dve.scalar_tensor_tensor(out=acc[:, s:T], in0=ps[:, 0:T - s], scalar=w[3 - s],
                                                  in1=acc[:, s:T], op0=ALU.mult, op1=ALU.add))
                read(dve.scalar_tensor_tensor(out=acc[:, 3:T], in0=ps[:, 0:T - 3], scalar=w[0],
                                              in1=acc[:, 3:T], op0=ALU.mult, op1=ALU.add), name)
                read_out(dve, name)
                dve.engine_nop().then_inc(S("qkv_conv"), 1)
            for j in range(8):
                read_out(dve, ("l2", j))
                dve.reciprocal(LRT[:, j % 2, :], LRT[:, j % 2, :]).then_inc(S("l2_recip"), 1)
                dve.wait_ge(S("l2_recip"), j + 1)
                dve.tensor_tensor(QKV[:, j, :], QKV[:, j, :], LRT[:, j % 2, :], ALU.mult).then_inc(S("qk_normed"), 1)
                dve.wait_ge(S("qk_normed"), j + 1)
                dve.engine_nop().then_inc(S("l2_inv"), 1)
            read_out(dve, "tok")
            for b in range(TB):
                for h in range(DN_H):
                    read_out(dve, ("rowb", 0, h))
                    dve.tensor_scalar(DT[:, b, h, :], GB[:, h, b * P:(b + 1) * P],
                                      TOK[:, 4 * b + h:4 * b + h + 1], 0.0, ALU.subtract, ALU.min)\
                       .then_inc(S("decay_arg"), 1)

            def tok(j, b):
                return TOK[:, 16 * j + 4 * b:16 * j + 4 * b + 4].unsqueeze(2).to_broadcast([P, DN_H, P])

            def h4(ps):
                return ps[:].rearrange("p (h i) -> p h i", h=DN_H)

            def head_bc(ap):
                return ap.unsqueeze(1).to_broadcast([P, DN_H, P])

            full(dve, "tok")
            for b in range(TB):
                at = slice(b * P, (b + 1) * P)
                ps = full(dve, ("kt", b))
                link(dve.tensor_tensor(KB[:, b, :, :], h4(ps), tok(2, b), ALU.mult))
                read(dve.tensor_tensor(KD[:, b, :, :], h4(ps), tok(3, b), ALU.mult), ("kt", b))
                ps = full(dve, ("vt", b))
                read(dve.tensor_tensor(VB[:, b, :, :], h4(ps), tok(1, b), ALU.mult), ("vt", b))
                dve.wait_ge(S("decay_exp"), b + 1)
                link(dve.tensor_tensor(DT[:, b, :, :], DT[:, b, :, :], head_bc(gd("causal")), ALU.mult))
                ps = full(dve, ("kk", b))
                read(dve.tensor_tensor(AT[:, b, :, :], h4(ps), DT[:, b, :, :], ALU.mult), ("kk", b))
                ps = full(dve, ("qk", b))
                read(dve.scalar_tensor_tensor(out=IN[:, b, :, :], in0=h4(ps), scalar=float(P) ** -0.5,
                                              in1=DT[:, b, :, :], op0=ALU.mult, op1=ALU.mult), ("qk", b))
                read_out(dve, ("kk", b))
                for h in range(DN_H):
                    read_out(dve, ("rowb", 2, h))
                dve.tensor_tensor(AT[:, b, :, :], AT[:, b, :, :], BB[:, :, at], ALU.mult).then_inc(S("a_done"), 1)
                dve.wait_ge(S("a_done"), b + 1)
                link(dve.tensor_tensor(TT[:, b, :, :], AT[:, b, :, :], head_bc(gd("level", 0, P)), ALU.mult))
                dve.scalar_tensor_tensor(out=TT[:, b, :, :], in0=TT[:, b, :, :], scalar=-1.0, in1=head_bc(ident),
                                         op0=ALU.mult, op1=ALU.add).then_inc(S("tt_start"), 1)
            full(dve, ("qk", TB - 1))
            for h in range(DN_H):
                read_out(dve, ("rowb", 1, h))
                dve.scalar_tensor_tensor(out=QKV[:, h, :], in0=QKV[:, h, :], scalar=float(P) ** -0.5,
                                         in1=EGB[:, h, :], op0=ALU.mult, op1=ALU.mult).then_inc(S("qdec_done"), 1)
            dve.memset(SS[:], 0.0).then_inc(S("state_zero"), 1)
            for lv in range(1, 6):
                for b in range(TB):
                    if lv < 5:
                        ps = full(dve, ("dt", lv, b))
                        if lv == 1:
                            read_out(dve, ("t0", b))
                        read(dve.tensor_tensor(TM[:, b, :, :], TM[:, b, :, :], h4(ps), ALU.subtract), ("dt", lv, b))
                    ps = full(dve, ("dtt", lv, b))
                    read(dve.tensor_tensor(TT[:, b, :, :], TT[:, b, :, :], h4(ps), ALU.subtract), ("dtt", lv, b))
            for c in range(8):
                b, r = c // 2, slice(CHUNK * (c % 2), CHUNK * (c % 2) + CHUNK)
                read_out(dve, ("u", b))
                ps = full(dve, ("ws", c))
                read(dve.tensor_tensor(VN[r, :, :], UU[r, b, :, :],
                                       ps[r, :].rearrange("p (h i) -> p h i", h=DN_H), ALU.subtract), ("ws", c))
                pk = full(dve, ("kv", c))
                if c:
                    full(dve, ("o", c - 1))
                for h in range(DN_H):
                    e = c * CHUNK + CHUNK - 1
                    dve.scalar_tensor_tensor(out=states[(c + 1) % 2][:, h, :], in0=states[c % 2][:, h, :],
                                             scalar=EGB[:, h, e:e + 1],
                                             in1=pk[:, h * P:(h + 1) * P], op0=ALU.mult, op1=ALU.add)\
                       .then_inc(S("state_done"), 1)
                dve.wait_ge(S("state_done"), 4 * c + 4)
                read(dve.engine_nop(), ("kv", c))
                if c == 2:
                    dve_mean(dve, "mem", 3, D, 2)
                if c == 5:
                    rs = dve_scale(dve, "mem", 3, 2)
                    for n in range(2):
                        dve.tensor_scalar(MEMN[:, n, :], MEMX[:, n, :], rs[:, n:n + 1], None, ALU.mult)\
                           .then_inc(S("mem_scaled"), 1)
            for h in range(DN_H):
                read_out(dve, ("on", h))
                link(dve.reciprocal(LRT[:, h % 2, :], LRT[:, h % 2, :]))
                dve.scalar_tensor_tensor(out=OT[:, h, :], in0=OT[:, h, :], scalar=V("dn_norm"),
                                         in1=LRT[:, h % 2, :], op0=ALU.mult, op1=ALU.mult).then_inc(S("on_inv"), 1)
                dve.wait_ge(S("on_inv"), h + 1)
                read_out(dve, (("proj", 6), h))
                dve.tensor_tensor(YT[:, 4 + h, :], OT[:, h, :], ZT[:, h, :], ALU.mult).then_inc(S("ydn_done"), 1)
            for c in range(KC):
                dve_low(dve, "memT", ("memT", c), MT[:, c, :], MTL[:, c, :], c, scale=V("norm_mem", c, c + 1))
            for n in range(2):
                for b in range(TB):
                    ps = full(dve, (("mo", n), b))
                    hs = H[:, b, n * 512:(n + 1) * 512]
                    read(dve.tensor_tensor(hs, hs, ps[:], ALU.add), (("mo", n), b))
            stage_end(dve, 1)
            rs = dve_norm_scale(dve, "x", 6, D)
            for b in range(TB):
                dve.tensor_scalar(XNX[:, b, :], H[:, b, :], rs[:, b:b + 1], None, ALU.mult).then_inc(S("x_scaled"), 1)
            for c in range(KC):
                dve_low(dve, "xT", ("xT", c), XT[:, c, :], XL2[:, c, :], c, scale=V("norm_x", c, c + 1))

            def x_scale(u):
                read_out(dve, ("xs", u))
                st = 160 + 8 * (u % 4)
                link(dve.reciprocal(stats[:, st + 4:st + 6], stats[:, st + 2:st + 4]))
                for h2 in range(2):
                    dve.tensor_scalar(XP[u % 4][:, h2, :], XP[u % 4][:, h2, :], stats[:, st + 4 + h2:st + 5 + h2],
                                      None, ALU.mult).then_inc(S("xp_ready"), 1)

            for u in range(8):
                ps = full(dve, ("xs", u))
                st = 160 + 8 * (u % 4)
                dve.tensor_reduce(stats[:, st:st + 2], ps[:].rearrange("p (h m) -> p h m", h=2), AXX, ALU.max,
                                  negate=True).then_inc(S("x_max"), 1)
                if u:
                    x_scale(u - 1)
            x_scale(7)
            for h in range(X_H):
                for dc in range(2):
                    c = 2 * h + dc
                    dve_low(dve, "xo", ("xo", h, dc), XO[:, c, :], XOL[:, c, :], c)
            for n in range(2):
                for b in range(TB):
                    ps = full(dve, (("xout", n), b))
                    hs = H[:, b, n * 512:(n + 1) * 512]
                    read(dve.tensor_tensor(hs, hs, ps[:], ALU.add), (("xout", n), b))
            rs = dve_norm_scale(dve, "peer", 9, D)
            stage_end(dve, 2)
            dve.wait_ge(S("gain_landed"), 16)
            for b in range(TB):
                dve.scalar_tensor_tensor(out=PX[:, b, :], in0=H[:, b, :], scalar=rs[:, b:b + 1], in1=GAIN,
                                         op0=ALU.mult, op1=ALU.mult).then_inc(S("peer_scaled"), 1)
            for c in range(KC):
                dve_low(dve, "pT", ("pT", c), XT[:, c, :], XL3[:, c, :], c)

            def topk(n):
                steps = [0]

                def step(ins):
                    ins.then_inc(S("topk_step"), 1)
                    steps[0] += 1

                def settled():
                    dve.wait_ge(S("topk_step"), n * TOPK_STEPS + steps[0])
                    dve.sem_inc(S("topk_turn"), 1)

                step(dve.tensor_copy(TS[:], SC[:, :, bass.ds(n * NKEY, NKEY)]))
                settled()
                for p in range(2):
                    step(dve.max(TV[:, p, 0:8], TS[:, p, :]))
                settled()
                for p in range(2):
                    step(dve.max_index(TI[:, p, 0:8], TV[:, p, 0:8], TS[:, p, :]))
                    step(dve.match_replace(TS2[:, p, :], TV[:, p, 0:8], TS[:, p, :], -3e38))
                settled()
                for p in range(2):
                    step(dve.max(TV[:, p, 8:16], TS2[:, p, :]))
                settled()
                for p in range(2):
                    step(dve.max_index(TI[:, p, 8:16], TV[:, p, 8:16], TS2[:, p, :]))
                step(dve.tensor_tensor(CAND[:], TV[:, 0, :].unsqueeze(2).to_broadcast([P, TOPK, TOPK]),
                                       TV[:, 1, :].unsqueeze(1).to_broadcast([P, TOPK, TOPK]), ALU.add))
                settled()
                step(dve.tensor_copy(TIF[:], TI[:]))
                step(dve.max(BEST[:, 0:8], CAND[:]))
                settled()
                step(dve.max_index(POS[:, 0:8], BEST[:, 0:8], CAND[:].rearrange("p a b -> p (a b)")))
                step(dve.match_replace(CAND2[:], BEST[:, 0:8], CAND[:], -3e38))
                step(dve.tensor_scalar(NB, BEST[:, 0:1], -1.0, None, ALU.mult))
                settled()
                dve.max(BEST[:, 8:16], CAND2[:]).then_inc(S("topk_best"), 1)
                dve.wait_ge(S("topk_best"), n + 1)
                dve.sem_inc(S("topk_turn"), 1)
                step(dve.max_index(POS[:, 8:16], BEST[:, 8:16], CAND2[:].rearrange("p a b -> p (a b)")))
                settled()
                step(dve.tensor_scalar(PAB[:, 0, :], POS, 4, None, ALU.logical_shift_right))
                step(dve.tensor_scalar(PAB[:, 1, :], POS, 15, None, ALU.bitwise_and))
                settled()
                step(dve.tensor_copy(PABF[:], PAB[:]))
                settled()
                iota = V("iota16").unsqueeze(1).to_broadcast([P, TOPK, TOPK])
                for p in range(2):
                    step(dve.tensor_tensor(EQ[:, p, :, :], PABF[:, p, :].unsqueeze(2).to_broadcast([P, TOPK, TOPK]),
                                           iota, ALU.is_equal))
                settled()
                for p in range(2):
                    step(dve.tensor_tensor(EQ[:, p, :, :], EQ[:, p, :, :],
                                           TIF[:, p, :].unsqueeze(1).to_broadcast([P, TOPK, TOPK]), ALU.mult))
                settled()
                step(dve.tensor_reduce(IJ[:], EQ[:], AXX, ALU.add))
                settled()
                step(dve.scalar_tensor_tensor(out=IDF, in0=IJ[:, 0, :], scalar=float(NKEY), in1=IJ[:, 1, :],
                                              op0=ALU.mult, op1=ALU.add))
                settled()
                step(dve.tensor_copy(IDX[:, bass.ds(n * TOPK, TOPK)], IDF))
                dve.wait_ge(S("topk_exp"), n + 1)
                step(dve.reciprocal(GINV, GSUM))
                settled()
                dve.tensor_scalar(GATE[:, bass.ds(n * TOPK, TOPK)], GE, GINV, None, ALU.mult)\
                   .then_inc(S("topk_done"), 1)
                dve.wait_ge(S("topk_done"), n + 1)
                assert steps[0] == TOPK_STEPS, steps

            def peer_dve(tb, i, ahead=True):
                for par in range(2):
                    g = 2 * i + (16 * tb + par)
                    for s in range(GROUP):
                        dve.wait_ge(S(f"u_landed{s}"), 16 * g + 16)
                        dve.tensor_tensor_reduce(UR[:, s, :], UR[:, s, :], PX[:, tb, :], 1.0, 0.0, ALU.mult, ALU.add,
                                                 DOTS[:, par, s:s + 1]).then_inc(S("dots_done"), 1)
                    dve.wait_ge(S("gelu_done"), g + 1)
                    dve.tensor_tensor(W8[:, par, :], ACTS[:, par, :],
                                      GATE[:, bass.ds(GROUP * g, GROUP)], ALU.mult)\
                       .then_inc(S("gated"), 1)
                if ahead:
                    topk(i + (PH * tb + AHEAD))
                for par in range(2):
                    g = 2 * i + (16 * tb + par)
                    dve.wait_ge(S("v_used"), GROUP * g + (GROUP + 1))
                    for k in range(2):
                        hs = H[:, tb, k * 512:(k + 1) * 512]
                        dve.tensor_tensor(hs, hs, psum[2 * par + k][:], ALU.add).then_inc(S("peer_added"), 1)
                    dve.wait_ge(S("peer_added"), 2 * g + 3)

            for hp in range(4):
                read_out(dve, ("ps", 0, hp))
            for n in range(AHEAD):
                topk(n)
            for b in range(1, TB):
                for hp in range(4):
                    read_out(dve, ("ps", b, hp))
            dve.sem_inc(S("dots_done"), 1)
            dve.sem_inc(S("peer_added"), 1)
            for tb in range(TB):
                with dve.Fori(0, PH if tb + 1 < TB else PH - AHEAD) as i:
                    peer_dve(tb, i)
            with dve.Fori(PH - AHEAD, PH) as i:
                peer_dve(TB - 1, i, ahead=False)
            rs = dve_norm_scale(dve, "final", 12, D)
            stage_end(dve, 3)
            dve.wait_ge(S("final_gain_landed"), 16)
            for b in range(TB):
                dve.scalar_tensor_tensor(out=H[:, b, :], in0=H[:, b, :], scalar=rs[:, b:b + 1], in1=FGAIN,
                                         op0=ALU.mult, op1=ALU.mult).then_inc(S("final_scaled"), 1)
            rs = dve_norm_scale(dve, "pre", 15, D)
            for b in range(TB):
                dve.tensor_scalar(XN2[:, b, :], H[:, b, :], rs[:, b:b + 1], None, ALU.mult)\
                   .then_inc(S("pre_scaled"), 1)
            for c in range(KC):
                dve_low(dve, "mT", ("mT", c), XT[:, c, :], XL4[:, c, :], c, scale=V("pre_mix", c, c + 1))
            dve.memset(HID[:], 0.0).then_inc(S("hid_zero"), 1)
            dve.memset(PC[:], 0.0).then_inc(S("hid_zero"), 1)
            dve.wait_ge(S("pos_landed"), 16)
            R = slice(64, 96)
            TWO_PI = (6.28125, 0.0019350051879882812, float(2 * np.pi - 6.28125 - 0.0019350051879882812))
            link(dve.tensor_copy(ANG[1][R, :], ANG[0][R, :].bitcast(I32)))
            link(dve.tensor_scalar(ANG[0][R, :], ANG[1][R, :], V("inv_freq")[R, :], None, ALU.mult))
            link(dve.tensor_scalar(ANG[1][R, :], ANG[0][R, :], float(1 / (2 * np.pi)), 12582912.0, ALU.mult, ALU.add))
            link(dve.tensor_scalar(ANG[1][R, :], ANG[1][R, :], 12582912.0, None, ALU.subtract))
            for part in TWO_PI:
                link(dve.scalar_tensor_tensor(out=ANG[0][R, :], in0=ANG[1][R, :], scalar=-part, in1=ANG[0][R, :],
                                              op0=ALU.mult, op1=ALU.add))
            PI_IN = 3.1415925
            link(dve.tensor_scalar(ANG[2][R, :], ANG[0][R, :], float(np.pi / 2), None, ALU.add))
            link(dve.tensor_scalar(ANG[1][R, :], ANG[2][R, :], float(np.pi), float(-2 * np.pi), ALU.is_gt, ALU.mult))
            link(dve.tensor_tensor(ANG[3][R, :], ANG[2][R, :], ANG[1][R, :], ALU.add))
            dve.tensor_scalar(ANG[3][R, :], ANG[3][R, :], PI_IN, -PI_IN, ALU.min, ALU.max).then_inc(S("angles"), 1)
            dve.tensor_scalar(ANG[0][R, :], ANG[0][R, :], PI_IN, -PI_IN, ALU.min, ALU.max).then_inc(S("angles"), 1)
            for j, name in enumerate(("pos_k", "pos_v")):
                read_out(dve, ("kv2", j))
                x = KX[:, j, :]
                first = x[:, 0:CMP_S * NCMP].rearrange("p (n l) -> p l n", l=CMP_S)
                second = x[:, CMP_S:CMP_S + CMP_S * NCMP].rearrange("p (n l) -> p l n", l=CMP_S)
                pos = V(name).unsqueeze(2).to_broadcast([P, CMP_L, NCMP])
                link(dve.tensor_tensor(PB[:, j, 0:CMP_S, :], first, pos[:, 0:CMP_S, :], ALU.add))
                dve.tensor_tensor(PB[:, j, CMP_S:CMP_L, :], second, pos[:, CMP_S:CMP_L, :], ALU.add)\
                   .then_inc(S("blocks_ready"), 1)
            for b in range(TB):
                read_out(dve, ("vwg", b))
            dve.wait_ge(S("att_landed"), 16)
            dve.wait_ge(S("hid_zero"), 2)
            read_out(dve, "ck1")
            for b in range(TB):
                st = 256 + 32 * (b % 2)
                if b >= 2:
                    full(dve, ("pcT", b - 2))
                for g in range(G):
                    ps = full(dve, ("cs", b, g))
                    for r in range(4):
                        h = 4 * g + r
                        ins = dve.tensor_tensor_reduce(PC[:, b % 2, h, 0:NCMP], ps[:, r * NCMP:(r + 1) * NCMP],
                                                       at_("cmp_dist", b * NCMP, (b + 1) * NCMP),
                                                       -(2.0 ** -(h + 1)), 3e38, ALU.add, ALU.min,
                                                       stats[:, st + h:st + h + 1])
                        ins.then_inc(S("cmp_min"), 1)
                    dve.wait_ge(S("cmp_min"), NH * b + 4 * g + 4)
                    read(dve.engine_nop(), ("cs", b, g))
                dve.wait_ge(S("cmp_exp"), NH * (b + 1))
                link(dve.reciprocal(stats[:, st + 16:st + 24], stats[:, st + 8:st + 16]))
                link(dve.tensor_tensor(stats[:, st + 24:st + 32], stats[:, st + 16:st + 24], GT[:, b, 0:NH], ALU.mult))
                link(dve.tensor_tensor(PC[:, b % 2, :, 0:NCMP], PC[:, b % 2, :, 0:NCMP],
                                       stats[:, st + 24:st + 32].unsqueeze(2).to_broadcast([P, NH, NCMP]), ALU.mult))
                dve.tensor_tensor(PC[:, b % 2, :, 0:NCMP], PC[:, b % 2, :, 0:NCMP],
                                  at_("cmp_mask", b * NCMP, (b + 1) * NCMP).unsqueeze(1)
                                  .to_broadcast([P, NH, NCMP]), ALU.mult).then_inc(S("pc_ready"), 1)

            def soft_min(name, u, b, mask, scale):
                ps = full(dve, (name, u))
                n = (b + 1) * P
                if u >= 4:
                    full(dve, ("nT" if name == "n" else "mT2", u - 4))
                dve.tensor_tensor_reduce(unit_rows(u)[:, 0:n], ps[:, 0:n], mask[:, T - n:T], -scale, 3e38,
                                         ALU.add, ALU.min, stats[:, 224 + 4 * (u % 4):225 + 4 * (u % 4)])\
                   .then_inc(S(name + "_min"), 1)
                dve.wait_ge(S(name + "_min"), u + 1)
                read(dve.engine_nop(), (name, u))

            def soft_scale(name, u, b, gate):
                dve.wait_ge(S(name + "_exp"), u + 1)
                st = 224 + 4 * (u % 4)
                link(dve.reciprocal(stats[:, st + 2:st + 3], stats[:, st + 1:st + 2]))
                p = unit_rows(u)[:, 0:(b + 1) * P]
                if gate is None:
                    ins = dve.tensor_scalar(p, p, stats[:, st + 2:st + 3], None, ALU.mult)
                else:
                    ins = dve.tensor_scalar(p, p, stats[:, st + 2:st + 3], gate, ALU.mult, ALU.mult)
                ins.then_inc(S(name + "_p"), 1)

            def n_gate(u):
                hb, b = divmod(u, TB)
                n, br = divmod(hb, 2)
                h = 4 * (n % 2) + n // 2
                return h, b, GT[:, b, NH * (1 + br) + h:NH * (1 + br) + h + 1]

            for u in range(64):
                h, b, gate = n_gate(u)
                soft_min("n", u, b, at_("negdist"), 2.0 ** -(h + 1))
                if u:
                    h, b, gate = n_gate(u - 1)
                    soft_scale("n", u - 1, b, gate)
            soft_scale("n", 63, 3, n_gate(63)[2])
            stage_end(dve, 4)
            R = slice(64, 96)
            for j, (a, b_, name) in enumerate(((0, 256, "cq"), (256, 384, "ckv"))):
                rs = dve_norm_scale(dve, name, 18 + 3 * j, b_ - a)
                for b in range(TB):
                    dve.tensor_scalar(CQ[:, b, a:b_], CQ[:, b, a:b_], rs[:, b:b + 1], None, ALU.mult)\
                       .then_inc(S("cq_scaled"), 1)
            dve.wait_ge(S("rope_table"), 2)
            def rope(h):
                src = KR if h == 0 else QM[:, h - 1, :]
                if h:
                    read_out(dve, ("uq", h - 1))
                ps = full(dve, ("rope", h))
                read(dve.tensor_tensor(RT[R, 0, :], ps[R, :], SIN[R, :], ALU.mult), ("rope", h))
                link(dve.tensor_tensor(RT[R, 1, :], src[R, :], COS[R, :], ALU.mult))
                read_out(dve, ("rope", h))
                if h == 0:
                    for k in range(NH):
                        link(dve.tensor_tensor(KM[R, k, :], RT[R, 0, :], RT[R, 1, :], ALU.add))
                    dve.sem_inc(S("k_roped"), NH)
                else:
                    dve.tensor_tensor(QM[R, h - 1, :], RT[R, 0, :], RT[R, 1, :], ALU.add).then_inc(S("q_roped"), 1)
                    dve.wait_ge(S("q_roped"), h)
            for h in range(3):
                rope(h)
            for u in range(32):
                if u % 4 == 0 and u // 4 + 3 <= NH:
                    rope(u // 4 + 3)
                soft_min("m", u, u % TB, at_("causal_neg"), 96.0 ** -0.5)
                if u:
                    soft_scale("m", u - 1, (u - 1) % TB, None)
            soft_scale("m", 31, 3, None)
            full(dve, ("mo2", NH - 1))

            def merged_low(c):
                dve.wait_ge(S("merged_high"), c + 1)
                dve.tensor_tensor(rounded(MG[:, c, :]), MG[:, c, :], rounded(MGH[:, c, :]).bitcast(F32),
                                  ALU.subtract)\
                   .then_inc(S("merged_low"), 1)

            for c in range(KC):
                ps = full(dve, ("bn", c))
                read(dve.tensor_tensor(MG[:, c, :], ps[:], GM[:, c, :], ALU.mult), ("bn", c))
                ps = full(dve, ("bm", c))
                read(dve.tensor_tensor(SB[:, 0, :], ps[:], GM[:, KC + c, :], ALU.mult), ("bm", c))
                read_out(dve, ("bn", c))
                read_out(dve, ("bm", c))
                dve.tensor_tensor(MG[:, c, :], MG[:, c, :], SB[:, 0, :], ALU.add).then_inc(S("merged"), 1)
                dve.wait_ge(S("merged"), c + 1)
                if c:
                    merged_low(c - 1)
            merged_low(KC - 1)
            rs = dve_norm_scale(dve, "post", 24, D)
            dve.wait_ge(S("post_gain_landed"), 16)
            for b in range(TB):
                link(dve.scalar_tensor_tensor(out=YB[:, b, :], in0=YB[:, b, :], scalar=rs[:, b:b + 1], in1=GA,
                                              op0=ALU.mult, op1=ALU.mult))
                dve.tensor_tensor(H[:, b, :], H[:, b, :], YB[:, b, :], ALU.add).then_inc(S("mix2_added"), 1)
            rs = dve_norm_scale(dve, "ffn", 12, D)
            stage_end(dve, 5)
            for b in range(TB):
                dve.tensor_scalar(FX[:, b, :], H[:, b, :], rs[:, b:b + 1], None, ALU.mult)\
                   .then_inc(S("ffn_scaled"), 1)
            for c in range(KC):
                dve_low(dve, "fT", ("fT", c), XT[:, c, :], XL5[:, c, :], c, scale=V("pre_ffn", c, c + 1))

            def up_product(n):
                for m in range(2):
                    dve.wait_ge(S("up_gelu"), 2 * n + m + 1)
                    dve.tensor_tensor(MF[:, 2 * n + m, :], AC[:, n % 2, m, :], AC[:, n % 2, 2 + m, :], ALU.mult)\
                       .then_inc(S("mf_ready"), 1)

            def up_low(n):
                for k in range(2 * n, 2 * n + 2):
                    dve.wait_ge(S("mf_high"), k + 1)
                    dve.tensor_tensor(rounded(MF[:, k, :]), MF[:, k, :], rounded(MFH(k)).bitcast(F32), ALU.subtract)\
                       .then_inc(S("mf_low"), 1)

            for n in range(11):
                for m in range(4):
                    c = 2 * n + m % 2 + FC * (m // 2)
                    name = (("up", n), m)
                    dve.wait_ge(S("up_affine"), 4 * n + m + 1)
                    ps = full(dve, name)
                    acc = AC[:, n % 2, m, :]
                    link(dve.scalar_tensor_tensor(out=acc[:, 1:T], in0=ps[:, 0:T - 1],
                                                  scalar=V("up_conv", 3 * c + 1, 3 * c + 2), in1=acc[:, 1:T],
                                                  op0=ALU.mult, op1=ALU.add))
                    dve.scalar_tensor_tensor(out=acc[:, 2:T], in0=ps[:, 0:T - 2],
                                             scalar=V("up_conv", 3 * c, 3 * c + 1), in1=acc[:, 2:T],
                                             op0=ALU.mult, op1=ALU.add).then_inc(S("up_conv"), 1)
                    dve.wait_ge(S("up_conv"), 4 * n + m + 1)
                    read(dve.engine_nop(), name)
                if n:
                    up_product(n - 1)
                if n >= 2:
                    up_low(n - 2)
            up_product(10)
            up_low(9)
            up_low(10)
            rs = dve_norm_scale(dve, "down", 15, D)
            dve.wait_ge(S("ffn_gain_landed"), 16)
            for b in range(TB):
                link(dve.scalar_tensor_tensor(out=YF[:, b, :], in0=YF[:, b, :], scalar=rs[:, b:b + 1], in1=GF,
                                              op0=ALU.mult, op1=ALU.mult))
                dve.tensor_tensor(H[:, b, :], H[:, b, :], YF[:, b, :], ALU.add).then_inc(S("ffn_added"), 1)
            stage_end(dve, 6)
            for c in range(KC):
                dve_low(dve, "hT", ("hT", c), XT[:, c, :], XL5[:, c, :], c)
            for n in range(2):
                for b in range(TB):
                    j = TB * n + b
                    read_out(dve, ("pg", n, b))
                    ps = full(dve, ("pe", n, b))
                    dve.tensor_tensor(YP[:, b, n * 512:(n + 1) * 512], ps[:], SG[:, j % 2, :], ALU.mult)\
                       .then_inc(S("ple_gated"), 1)
                    dve.wait_ge(S("ple_gated"), j + 1)
                    read(dve.engine_nop(), ("pe", n, b))
            rs = dve_norm_scale(dve, "ple", 18, D)
            dve.wait_ge(S("ple_gain_landed"), 16)
            for b in range(TB):
                link(dve.scalar_tensor_tensor(out=YP[:, b, :], in0=YP[:, b, :], scalar=rs[:, b:b + 1], in1=GP,
                                              op0=ALU.mult, op1=ALU.mult))
                dve.tensor_tensor(H[:, b, :], H[:, b, :], YP[:, b, :], ALU.add).then_inc(S("out_ready"), 1)

        @block.gpsimd
        def _(pool):
            pool.wait_ge(S("vec_landed"), 16)
            split_weights(pool, SPLIT_STAGES[0][:14])
            pool.wait_ge(S("gdn_landed"), 16)
            for lv in range(1, 6):
                for b in range(TB):
                    if lv == 1:
                        pool.wait_ge(S("a_done"), TB)
                    else:
                        full(pool, ("x", lv - 1, b))
                    pool.tensor_tensor(CM[:, b, :].rearrange("p (h i) -> p h i", h=DN_H), AT[:, b, :, :],
                                       gd("level", lv * P, (lv + 1) * P).unsqueeze(1).to_broadcast([P, DN_H, P]),
                                       ALU.mult).then_inc(S("c_masked"), 1)
            for k in range(8):
                if k == 4:
                    split_weights(pool, SPLIT_STAGES[0][14:14 + SLOTS])
                pool.wait_ge(S("y_high"), k + 1)
                pool.tensor_tensor(rounded(YT[:, k, :]), YT[:, k, :], rounded(YH(k)).bitcast(F32), ALU.subtract)\
                    .then_inc(S("y_low"), 1)
            split_weights(pool, SPLIT_STAGES[0][14 + SLOTS:])
            split_weights(pool, SPLIT_STAGES[1])
            split_weights(pool, SPLIT_STAGES[2])

            def take_indices(g, buf):
                pool.tensor_copy(IG[:, buf, :], IDX[:, bass.ds(GROUP * g, GROUP)]).then_inc(S("indices_taken"), 1)

            def peer_pool(i, last=False):
                for par in range(2):
                    g = 2 * i + par
                    pool.wait_ge(S("indices_taken"), g + 1)
                    pool.sem_inc(S("pool_turn"), 1)
                    for s in range(GROUP):
                        pool.wait_ge(S("dots_done"), GROUP * g + 1)
                        pool.sem_inc(S("pool_turn"), 1)
                        pool.indirect_dma_start(UR[:, s, :], None, io["expert_u"],
                                                bass.IndirectOffsetOnAxis(IG[:, par, s:s + 1], 0))\
                            .then_inc(S(f"u_landed{s}"), 16)
                    if not (last and par):
                        pool.wait_ge(S("v_used"), GROUP * g + 1)
                        if par:
                            pool.wait_ge(S("topk_done"), i + 2)
                        pool.sem_inc(S("pool_turn"), 1)
                        take_indices(g + 1, 1 - par)
                    for s in range(GROUP):
                        pool.wait_ge(S("v_used"), GROUP * g + 1)
                        pool.sem_inc(S("pool_turn"), 1)
                        pool.indirect_dma_start(VR[:, s, :], None, io["expert_v"],
                                                bass.IndirectOffsetOnAxis(IG[:, par, s:s + 1], 0))\
                            .then_inc(S(f"v_landed{s}"), 16)

            full(pool, ("ps", TB - 1, 3))
            pool.wait_ge(S("topk_done"), 1)
            take_indices(0, 0)
            with pool.Fori(0, TB * PH - 1) as i:
                peer_pool(i)
            peer_pool(TB * PH - 1, last=True)
            split_weights(pool, SPLIT_STAGES[3])
            split_weights(pool, SPLIT_STAGES[4])
            split_weights(pool, SPLIT_STAGES[5])
            split_weights(pool, SPLIT_STAGES[6])

        @block.sync
        def _(sp):
            def weights(names):
                for name in names:
                    n = TILE_NO[name]
                    if n >= SLOTS:
                        s, v = tile_free[WEIGHT_TILES[n - SLOTS][0]]
                        sp.wait_ge(s, v)
                    at, w = TILE_AT[name], WEIGHT_TILES[n][1]
                    sp.dma_start(ring[:, n % SLOTS, 0:w],
                                 io["stream"][at:at + P * w].rearrange("(p f) -> p f", f=w))\
                      .then_inc(S(f"weights_landed{n % SLOTS}"), 16)

            names = [n for n, _ in WEIGHT_TILES]
            given = [0]

            def weights_to(name):
                end = names.index(name) + 1
                weights(names[given[0]:end])
                given[0] = end

            sp.dma_start(H[:], io["x"].rearrange("(b p) d -> p b d", p=P)).then_inc(S("x_landed"), 16)
            sp.dma_start(vec[:], io["vec"]).then_inc(S("vec_landed"), 16)
            weights_to("w_in2")
            sp.dma_start(gdn, io["gdn"]).then_inc(S("gdn_landed"), 16)
            weights_to("w_out1_0")
            full(sp, ("u", TB - 1))
            sp.dma_start(MEMX[:], io["mem"].rearrange("(b p) d -> p b d", p=P)).then_inc(S("mem_landed"), 16)
            weights_to("w_out1_1")
            weights_to("w_xq2")
            full(sp, (("xv", 1), 1))
            sp.dma_start(GAIN, io["norm_ffn"].rearrange("a d -> (a d)").partition_broadcast(P))\
              .then_inc(S("gain_landed"), 16)
            weights_to("w_xo1_1")
            weights_to("w_pq2")
            weights_to("peer_keys")
            weights_to("w2_kv0")
            full(sp, ("ps", TB - 1, 3))
            sp.dma_start(FGAIN, io["norm_final"].rearrange("a d -> (a d)").partition_broadcast(P))\
              .then_inc(S("final_gain_landed"), 16)
            sp.wait_ge(S("stage_end"), STAGE_ENGINES * 3)
            sp.dma_start(SIN[64:96, :], io["positions"].rearrange("a d -> (a d)").bitcast(F32)
                         .partition_broadcast(ROPE)).then_inc(S("pos_landed"), 16)
            sp.dma_start(att, io["att"]).then_inc(S("att_landed"), 16)
            weights_to("w2_merge7")
            sp.dma_start(GA, io["post_mix"].rearrange("a d -> (a d)").partition_broadcast(P))\
              .then_inc(S("post_gain_landed"), 16)
            weights_to("w_o1_1")
            weights_to("w_down0_2")
            sp.wait_ge(S("mf_ready"), FC)
            for dst, name, sem in ((GF, "post_ffn", "ffn_gain_landed"), (GP, "g_ple", "ple_gain_landed")):
                sp.dma_start(dst, io[name].rearrange("a d -> (a d)").partition_broadcast(P)).then_inc(S(sem), 16)
            sp.dma_start(PI[:], io["ple"].rearrange("(b p) d -> p b d", p=P)).then_inc(S("ple_landed"), 16)
            weights_to(names[-1])
            for b in range(TB):
                sp.wait_ge(S("out_ready"), b + 1)
                sp.dma_start(io["out"][b * P:(b + 1) * P, :], H[:, b, :]).then_inc(S("out_stored"), 16)
            sp.wait_ge(S("out_stored"), 16 * TB)


def constants():
    p = np.arange(P)
    f = np.float32
    c = {"ident": np.eye(P, dtype=f), "ones": np.ones((P, P), f), "eps": np.full((P, 1), EPS, f)}
    same = (p[:, None] // CHUNK) == (p[None, :] // CHUNK)
    c["causal"] = ((p[None, :] >= p[:, None]) & same).astype(f)
    lv = []
    for s in LEVELS:
        block = p[:, None] // (2 * s) == p[None, :] // (2 * s)
        lv.append((block & (p[None, :] // s % 2 == 1) & (p[:, None] // s % 2 == 0)).astype(f))
    c["level"] = np.concatenate(lv, 1)
    pick = np.zeros((P, DN_H, P), f)
    for h in range(DN_H):
        pick[h, h] = 1
    c["pick"] = pick.reshape(P, -1)
    c["restart"] = np.broadcast_to((np.arange(T) % CHUNK != 0).astype(f), (P, T))
    c["iota16"] = np.broadcast_to(np.arange(TOPK, dtype=f), (P, TOPK))
    slopes = np.array([2.0 ** (-8.0 * (i + 1) / NH) for i in range(NH)], dtype=f)
    qs = np.zeros((P, 4), f)
    for m in range(4):
        qs[0:64, m] = DH ** -0.5 / slopes[m]
        qs[64:128, m] = DH ** -0.5 / slopes[4 + m]
    c["q_scale"] = qs
    inv = (10000.0 ** (-np.arange(0, ROPE, 2, dtype=f) / f(ROPE))).astype(f)
    c["inv_freq"] = inv[p % 16][:, None]
    rot = np.zeros((P, ROPE), f)
    for m in range(16):
        rot[64 + 16 + m, m] = -1
        rot[64 + m, 16 + m] = 1
    c["rot"] = rot
    dist = p[:, None] + 384 - np.arange(T)[None, :]
    c["negdist"] = np.where(dist >= 0, -dist, NEG).astype(f)
    c["causal_neg"] = np.where(dist >= 0, 0.0, NEG).astype(f)
    t = np.arange(TB)[None, :, None] * P + p[:, None, None]
    dc = t - (np.arange(NCMP) * CMP_S + CMP_L - 1)[None, None, :]
    c["cmp_dist"] = np.where(dc >= 0, -dc, NEG).astype(f).reshape(P, -1)
    c["cmp_mask"] = (dc >= 0).astype(f).reshape(P, -1)
    return c


def columns(v):
    return np.ascontiguousarray(v.reshape(-1, P).T)


def rows_tile(w):
    k = w.shape[0] // P
    return w.reshape(k, P, -1).transpose(1, 0, 2).reshape(P, -1)


def lay_out(i):
    a = {k: np.asarray(v) for k, v in i.items()}
    f = np.float32
    c = constants()

    def twice(x):
        return np.concatenate([x, x], 0)

    def four(v):
        out = np.zeros((P, 1), f)
        out[0:4, 0] = v
        return out

    def diagonal(w):
        out = np.zeros((2, 64, w.shape[0], 2, 64), f)
        for g in range(2):
            out[g, :, :, g, :] = w.transpose(1, 0, 2)
        return out.reshape(P, -1)

    w_in, w2 = a["w_in"][0], a["w_in_2"][0]
    c |= {
        "norm_mix": columns(a["norm_mix"][0]), "norm_mem": columns(a["norm_mem"][0]),
        "norm_x": columns(a["norm_x"][0]),
        "conv_w": a["conv_w"][0].reshape(CONV_K, 4, P).transpose(2, 1, 0).reshape(P, -1),
        "dn_conv_w": a["dn_conv_w"][0].reshape(DN_CONV_K, 12, P).transpose(2, 1, 0).reshape(P, -1),
        "dn_norm": a["dn_norm"][0][:, None], "a_log": four(a["dn_a_log"][0]), "dt_bias": four(a["dn_dt_bias"][0]),
        "w_ba": rows_tile(w_in[:, 3584:3592]),
        "pre_mix": columns(a["g_pre_mix_2"][0]), "pre_ffn": columns(a["g_pre_ffn_2"][0]),
        "ck_b1": twice(a["nsa_ck_b1_2"][0][:, None]), "cv_b1": twice(a["nsa_cv_b1_2"][0][:, None]),
        "pos_k": twice(a["nsa_pos_k_2"][0].T), "pos_v": twice(a["nsa_pos_v_2"][0].T),
        "ck_w2": diagonal(a["nsa_ck_w2_2"]), "cv_w2": diagonal(a["nsa_cv_w2_2"]),
        "g_q": columns(a["mla_g_q_2"][0]), "g_kv": columns(a["mla_g_kv_2"][0]),
        "up_conv": a["w_conv_2"][0].reshape(3, 2 * FC, P).transpose(2, 1, 0).reshape(P, -1),
        "up_b": columns(a["b_conv_2"][0]),
    }

    def pack(spec):
        return np.concatenate([np.asarray(c[n], f).reshape(P, w) for n, w in spec], 1)

    t = {}

    def columns_of(name, w):
        for n in range(w.shape[1] // 256):
            t[f"{name}{n}"] = rows_tile(w[:, n * 256:(n + 1) * 256])

    def rows_of(name, w, rows=(4, 4)):
        for n in range(2):
            at = 0
            for k, r in enumerate(rows):
                t[f"{name}{n}_{k}"] = rows_tile(w[at * P:(at + r) * P, n * 512:(n + 1) * 512])
                at += r

    columns_of("w_in", w_in[:, 0:3584])
    for name, w in (("w_xk", a["w_xkv"][0][:, :D]), ("w_xq", a["w_xq"][0]), ("w_pq", a["w_pq"][0])):
        columns_of(name, w)
    for name, w in (("w_out", a["w_out"][0]), ("w_xv", a["w_xkv"][0][:, D:]), ("w_xo", a["w_xo"][0]),
                    ("w_o", a["w_o_2"][0]), ("w_pg", a["w_ple_gate_2"][0])):
        rows_of(name, w)
    t["peer_keys"] = a["peer_keys"][0].transpose(1, 3, 0, 2).reshape(P, -1)
    columns_of("w2_q", w2[:, 0:512].reshape(D, 2, 4, 64).transpose(0, 2, 1, 3).reshape(D, 512))
    columns_of("w2_kv", w2[:, 512:1024])
    t["w2_kw"] = rows_tile(w2[:, 1024:1152])
    t["w2_vwg"] = rows_tile(w2[:, 1152:1304])
    for k in range(2):
        t[f"w2_cq_{k}"] = rows_tile(w2[k * 512:(k + 1) * 512, 1304:1688])
    t["w2_kr"] = rows_tile(np.concatenate([np.zeros((D, 64), f), w2[:, 1688:1720]], 1))
    t["ck_w1"] = diagonal(a["nsa_ck_w1_2"][0].reshape(CMP_L, 64, 64))
    t["cv_w1"] = diagonal(a["nsa_cv_w1_2"][0].reshape(CMP_L, 64, 64))
    columns_of("w2_merge", w2[:, 1720:])
    t["w_uq"] = rows_tile(a["mla_w_uq_2"][0])
    t["w_ukv"] = rows_tile(a["mla_w_ukv_2"][0])
    t["w_br_nsa"] = rows_tile(a["w_br_nsa_2"][0].reshape(2, 4, 64, D).transpose(1, 0, 2, 3).reshape(512, D))
    t["w_br_mla"] = rows_tile(a["w_br_mla_2"][0])
    up = a["w_up_2"][0]
    columns_of("w_up", up.reshape(D, 2, 11, 256).transpose(0, 2, 1, 3).reshape(D, 2 * DFF))
    rows_of("w_down", a["w_down_2"][0], DOWN_ROWS)
    for n in range(2):
        t[f"w_ple{n}"] = rows_tile(a["w_ple_2"][0][:, n * 512:(n + 1) * 512])
    for name, w in WEIGHT_TILES:
        assert t[name].shape == (P, w), (name, t[name].shape, w)
    stream = np.concatenate([t[name].reshape(-1) for name, _ in WEIGHT_TILES])
    return {
        "x": a["x"][0], "mem": a["mem"][0], "vec": pack(VEC), "gdn": pack(GDN), "att": pack(ATT), "stream": stream,
        "expert_u": a["expert_u"][0], "expert_v": a["expert_v"][0], "norm_ffn": a["norm_ffn"],
        "norm_final": a["norm_final"][None], "post_mix": a["g_post_mix_2"], "post_ffn": a["g_post_ffn_2"],
        "g_ple": a["g_ple_2"], "ple": a["p_2"][0, 0], "positions": a["positions_2"],
    }


def kernel(**inputs):
    import concourse.bacc as bacc
    from concourse.bass_utils import run_bass_kernel_spmd
    nc = bacc.Bacc("TRN2", target_bir_lowering=False, num_devices=1)
    arrays = {k: np.ascontiguousarray(v) for k, v in lay_out(inputs).items()}
    io = {k: nc.dram_tensor(f"in_{k}", v.shape, mybir.dt.from_np(v.dtype), kind="ExternalInput").ap()
          for k, v in arrays.items()}
    io["out"] = nc.dram_tensor("out_0", (T, D), F32, kind="ExternalOutput").ap()
    build(nc, io)
    r = run_bass_kernel_spmd(nc, [{f"in_{k}": v for k, v in arrays.items()}], core_ids=[0])
    return r.results[0]["out_0"].reshape(1, T, D)
```
